# Optimizing a Trainium2 kernel written in Bass

```python
import math
import jax, jax.numpy as jnp
from jax import lax
import numpy as np

D_MODEL = 2048
BATCH = 1
SEQ = 256
DEPTH = 1

CHUNK = 64
N_MEM = 256
N_BRANCH = 3
D_CONV = D_MODEL // 2
CONV_WIDTH = 31
ATTN_HEAD_DIM = 64
D_ATTN = D_MODEL // 2
N_ATTN_HEADS = D_ATTN // ATTN_HEAD_DIM
LEFT_CHUNKS = 8
BAND = LEFT_CHUNKS + 1
MAX_REL = 256
N_MEM_HEADS = 4
D_MEM = D_MODEL // 2
MEM_HEAD_DIM = D_MEM // N_MEM_HEADS
D_FF = ((8 * D_MODEL // 3 + 255) // 256) * 256
FFN_CONV_WIDTH = 3
D_IN = 2 * D_CONV + 3 * D_ATTN + D_MEM + N_BRANCH * D_MODEL
SPLITS = (2 * D_CONV, 2 * D_CONV + 3 * D_ATTN, 2 * D_CONV + 3 * D_ATTN + D_MEM)
EPS = 1e-6
NEG_INF = -1e30


def rmsnorm(x, g):
    xf = x.astype(jnp.float32)
    y = xf * lax.rsqrt(jnp.mean(xf * xf, axis=-1, keepdims=True) + EPS)
    return (y * g.astype(jnp.float32)).astype(x.dtype)

def layernorm(x, g, b):
    xf = x.astype(jnp.float32)
    mu = jnp.mean(xf, axis=-1, keepdims=True)
    var = jnp.mean(jnp.square(xf - mu), axis=-1, keepdims=True)
    y = (xf - mu) * lax.rsqrt(var + EPS)
    return (y * g.astype(jnp.float32) + b.astype(jnp.float32)).astype(x.dtype)

def causal_dwconv(x, w, b):
    width = w.shape[0]
    ch = x.shape[-1]
    y = lax.conv_general_dilated(
        x, w[:, None, :].astype(x.dtype), window_strides=(1,),
        padding=[(width - 1, 0)], dimension_numbers=('NWC', 'WIO', 'NWC'),
        feature_group_count=ch)
    return y + b.astype(x.dtype)

def conv_module(u, conv_w, conv_b, ln_g, ln_b):
    a, gt = jnp.split(u, 2, axis=-1)
    h = a * jax.nn.sigmoid(gt)
    h = causal_dwconv(h, conv_w, conv_b)
    return jax.nn.silu(layernorm(h, ln_g, ln_b))

def chunk_attention(q, k, v, rel_bias):
    b, s, h, hd = q.shape
    nc = s // CHUNK
    qc = q.reshape(b, nc, CHUNK, h, hd)
    pad = ((0, 0), (LEFT_CHUNKS, 0), (0, 0), (0, 0), (0, 0))
    kp = jnp.pad(k.reshape(b, nc, CHUNK, h, hd), pad)
    vp = jnp.pad(v.reshape(b, nc, CHUNK, h, hd), pad)
    band_idx = jnp.arange(nc)[:, None] + jnp.arange(BAND)[None, :]
    kb = kp[:, band_idx].reshape(b, nc, BAND * CHUNK, h, hd)
    vb = vp[:, band_idx].reshape(b, nc, BAND * CHUNK, h, hd)
    scores = jnp.einsum('bcqhd,bckhd->bhcqk', qc, kb).astype(jnp.float32) * (hd ** -0.5)
    qi = jnp.arange(CHUNK)[:, None]
    km = jnp.arange(BAND * CHUNK)[None, :]
    dist = LEFT_CHUNKS * CHUNK + qi - km
    rel_idx = jnp.clip(dist, -MAX_REL, MAX_REL) + MAX_REL
    bias = rel_bias.astype(jnp.float32)[:, rel_idx]
    valid = jnp.repeat(band_idx >= LEFT_CHUNKS, CHUNK, axis=1)
    scores = scores + bias[None, :, None, :, :]
    scores = jnp.where(valid[None, None, :, None, :], scores, NEG_INF)
    p = jax.nn.softmax(scores, axis=-1).astype(v.dtype)
    out = jnp.einsum('bhcqk,bckhd->bcqhd', p, vb)
    return out.reshape(b, s, h * hd)

def memory_attention(q, km, vm):
    b, s, h, hd = q.shape
    scores = jnp.einsum('bshd,bmhd->bhsm', q, km).astype(jnp.float32) * (hd ** -0.5)
    p = jax.nn.softmax(scores, axis=-1).astype(vm.dtype)
    out = jnp.einsum('bhsm,bmhd->bshd', p, vm)
    return out.reshape(b, s, h * hd)

def first_inputs(seed: int = 0) -> dict:
    key = jax.random.key(seed)
    ks = jax.random.split(key, 24)

    def nrm(k, shape, scale):
        return jax.random.normal(k, shape, jnp.float32) * scale

    def gain(k, shape):
        return 1.0 + 0.05 * jax.random.normal(k, shape, jnp.float32)

    L = DEPTH
    return {
        'x': nrm(ks[0], (BATCH, SEQ, D_MODEL), 1.0),
        'mem': nrm(ks[1], (BATCH, N_MEM, D_MODEL), 1.0),
        'mix_norm_g': gain(ks[2], (L, D_MODEL)),
        'mem_norm_g': gain(ks[3], (L, D_MODEL)),
        'w_in': nrm(ks[4], (L, D_MODEL, D_IN), D_MODEL ** -0.5),
        'gate_b': nrm(ks[5], (L, N_BRANCH * D_MODEL), 0.1),
        'conv_w': nrm(ks[6], (L, CONV_WIDTH, D_CONV), CONV_WIDTH ** -0.5),
        'conv_b': nrm(ks[7], (L, D_CONV), 0.02),
        'conv_ln_g': gain(ks[8], (L, D_CONV)),
        'conv_ln_b': nrm(ks[9], (L, D_CONV), 0.02),
        'w_conv_out': nrm(ks[10], (L, D_CONV, D_MODEL), D_CONV ** -0.5),
        'rel_bias': nrm(ks[11], (L, N_ATTN_HEADS, 2 * MAX_REL + 1), 0.1),
        'w_attn_out': nrm(ks[12], (L, D_ATTN, D_MODEL), D_ATTN ** -0.5),
        'w_mem_kv': nrm(ks[13], (L, D_MODEL, 2 * D_MEM), D_MODEL ** -0.5),
        'w_mem_out': nrm(ks[14], (L, D_MEM, D_MODEL), D_MEM ** -0.5),
        'w_o': nrm(ks[15], (L, D_MODEL, D_MODEL), D_MODEL ** -0.5),
        'ffn_norm_g': gain(ks[16], (L, D_MODEL)),
        'w_up': nrm(ks[17], (L, D_MODEL, 2 * D_FF), D_MODEL ** -0.5),
        'ffn_conv_w': nrm(ks[18], (L, FFN_CONV_WIDTH, 2 * D_FF), FFN_CONV_WIDTH ** -0.5),
        'ffn_conv_b': nrm(ks[19], (L, 2 * D_FF), 0.02),
        'w_down': nrm(ks[20], (L, D_FF, D_MODEL), D_FF ** -0.5),
        'final_norm_g': gain(ks[21], (D_MODEL,)),
    }

def first_block(x, mem, mix_norm_g, mem_norm_g, w_in, gate_b, conv_w, conv_b, conv_ln_g, conv_ln_b,
              w_conv_out, rel_bias, w_attn_out, w_mem_kv, w_mem_out, w_o, ffn_norm_g, w_up,
              ffn_conv_w, ffn_conv_b, w_down, final_norm_g):
    b, s, d = x.shape
    h = x
    for l in range(DEPTH):
        xn = rmsnorm(h, mix_norm_g[l])
        proj = xn @ w_in[l]
        u_conv, qkv, q_mem, gates = jnp.split(proj, SPLITS, axis=-1)
        y_conv = conv_module(u_conv, conv_w[l], conv_b[l], conv_ln_g[l], conv_ln_b[l]) @ w_conv_out[l]
        q, k, v = jnp.split(qkv.reshape(b, s, 3, N_ATTN_HEADS, ATTN_HEAD_DIM), 3, axis=2)
        y_attn = chunk_attention(q[:, :, 0], k[:, :, 0], v[:, :, 0], rel_bias[l]) @ w_attn_out[l]
        mn = rmsnorm(mem, mem_norm_g[l])
        kv = (mn @ w_mem_kv[l]).reshape(b, mem.shape[1], 2, N_MEM_HEADS, MEM_HEAD_DIM)
        qm = q_mem.reshape(b, s, N_MEM_HEADS, MEM_HEAD_DIM)
        y_mem = memory_attention(qm, kv[:, :, 0], kv[:, :, 1]) @ w_mem_out[l]
        g = jax.nn.sigmoid(gates + gate_b[l]).reshape(b, s, N_BRANCH, d)
        merged = g[:, :, 0] * y_conv + g[:, :, 1] * y_attn + g[:, :, 2] * y_mem
        h = h + merged @ w_o[l]
        hn = rmsnorm(h, ffn_norm_g[l])
        up = causal_dwconv(hn @ w_up[l], ffn_conv_w[l], ffn_conv_b[l])
        val, gt = jnp.split(up, 2, axis=-1)
        h = h + (jax.nn.silu(gt) * val) @ w_down[l]
    return rmsnorm(h, final_norm_g)


HEAD_DIM = 64
N_MIXERS = 4
HEADS_PER_MIXER = 8
GROUP_WIDTH = HEADS_PER_MIXER * HEAD_DIM
MIX_WIDTH = N_MIXERS * GROUP_WIDTH
N_HEADS_TOTAL = N_MIXERS * HEADS_PER_MIXER
SCALE = HEAD_DIM ** -0.5

REL_BUCKETS = 32
REL_MAX_DIST = 2048

DILATED_CONFIGS = ((128, 1), (512, 4), (2048, 16))

SWA_WINDOW = 128
SWA_KV_HEADS = 2

MOBA_BLOCK = 256
MOBA_TOPK = 3

NSA_KV_HEADS = 2
NSA_CMP_BLOCK = 32
NSA_CMP_STRIDE = 16
NSA_CMP_HIDDEN = 128
NSA_SLC_BLOCK = 64
NSA_SLC_TOPN = 16
NSA_WINDOW = 512

BAND_BLOCK = 128
QUERY_CHUNK = 64

N_EXPERTS = 16
N_EXPERT_GROUPS = 4
TOPK_GROUPS = 1
TOPK_EXPERTS = 2
D_EXPERT = 512

NORM_EPS = 1e-6
NEG_INF_2 = -1e30

KV_B = SWA_KV_HEADS * HEAD_DIM
KV_D = NSA_KV_HEADS * HEAD_DIM
IN_SIZES = (GROUP_WIDTH, GROUP_WIDTH, GROUP_WIDTH,
            GROUP_WIDTH, KV_B, KV_B,
            GROUP_WIDTH, GROUP_WIDTH, GROUP_WIDTH,
            GROUP_WIDTH, KV_D, KV_D, KV_D, KV_D, KV_D, KV_D, HEADS_PER_MIXER * 3)
IN_COLS = sum(IN_SIZES)


def rmsnorm_2(x, g):
    xf = x.astype(jnp.float32)
    ms = jnp.mean(xf * xf, axis=-1, keepdims=True)
    return (xf * lax.rsqrt(ms + NORM_EPS)).astype(x.dtype) * g

def t5_bucket(dist):
    dist = jnp.maximum(dist, 0)
    max_exact = REL_BUCKETS // 2
    large = max_exact + (jnp.log(jnp.maximum(dist, 1).astype(jnp.float32) / max_exact)
                         / math.log(REL_MAX_DIST / max_exact) * (REL_BUCKETS - max_exact)).astype(jnp.int32)
    large = jnp.minimum(large, REL_BUCKETS - 1)
    return jnp.where(dist < max_exact, dist, large)

def masked_softmax(s, mask, sink=None):
    s = jnp.where(mask, s, NEG_INF_2)
    m = jnp.max(s, axis=-1, keepdims=True)
    if sink is not None:
        m = jnp.maximum(m, sink)
    e = jnp.where(mask, jnp.exp(s - m), 0.0)
    den = jnp.sum(e, axis=-1, keepdims=True)
    if sink is not None:
        den = den + jnp.exp(sink - m)
    den = jnp.maximum(den, jnp.finfo(jnp.float32).tiny)
    return e / den, (m + jnp.log(den))[..., 0]

def banded_attention(q, k, v, max_dist, tab, dist_scale, sink=None):
    b, hk, g, L, hd = q.shape
    nblk = -(-L // BAND_BLOCK)
    Lp = nblk * BAND_BLOCK
    nprev = -(-max_dist // BAND_BLOCK)
    nk = (nprev + 1) * BAND_BLOCK
    q = jnp.pad(q, ((0, 0), (0, 0), (0, 0), (0, Lp - L), (0, 0)))
    pad_kv = ((0, 0), (0, 0), (nprev * BAND_BLOCK, Lp - L), (0, 0))
    k = jnp.pad(k, pad_kv)
    v = jnp.pad(v, pad_kv)
    kidx = np.arange(nblk)[:, None] * BAND_BLOCK + np.arange(nk)[None, :]
    kb = k[:, :, kidx]
    vb = v[:, :, kidx]
    qb = q.reshape(b, hk, g, nblk, BAND_BLOCK, hd)
    rel = np.arange(BAND_BLOCK)[:, None] + nprev * BAND_BLOCK - np.arange(nk)[None, :]
    kpos = np.arange(nblk)[:, None, None] * BAND_BLOCK - nprev * BAND_BLOCK + np.arange(nk)[None, None, :]
    mask = (rel >= 0) & (rel <= max_dist) & (kpos >= 0)
    bias = tab.astype(jnp.float32)[:, :, t5_bucket(jnp.asarray(rel * dist_scale))]
    s = jnp.einsum('bhgnqd,bhnkd->bhgnqk', qb, kb).astype(jnp.float32) * SCALE + bias[None, :, :, None]
    if sink is not None:
        sink = sink.astype(jnp.float32)[None, :, :, None, None, None]
    p, lse = masked_softmax(s, mask, sink)
    o = jnp.einsum('bhgnqk,bhnkd->bhgnqd', p.astype(v.dtype), vb).reshape(b, hk, g, Lp, hd)[:, :, :, :L]
    return o, lse.reshape(b, hk, g, Lp)[:, :, :, :L]

def dilated_attention(q, k, v, tab):
    b, h, s, hd = q.shape
    outs, lses = [], []
    for window, r in DILATED_CONFIGS:
        def strided(t):
            return t.reshape(b, h, s // r, r, hd).transpose(0, 3, 1, 2, 4).reshape(b * r, h, s // r, hd)
        o, lse = banded_attention(strided(q)[:, :, None], strided(k), strided(v), window // r, tab[:, None], r)
        outs.append(o[:, :, 0].reshape(b, r, h, s // r, hd).transpose(0, 2, 3, 1, 4).reshape(b, h, s, hd))
        lses.append(lse[:, :, 0].reshape(b, r, h, s // r).transpose(0, 2, 3, 1).reshape(b, h, s))
    w = jax.nn.softmax(jnp.stack(lses, axis=0), axis=0)
    o = w[0][..., None] * outs[0] + w[1][..., None] * outs[1] + w[2][..., None] * outs[2]
    return o.astype(q.dtype)

def moba_attention(q, k, v, tab):
    b, h, s, hd = q.shape
    nb = -(-s // MOBA_BLOCK)
    sp = nb * MOBA_BLOCK
    pad = ((0, 0), (0, 0), (0, sp - s), (0, 0))
    q, k, v = jnp.pad(q, pad), jnp.pad(k, pad), jnp.pad(v, pad)
    kb = k.reshape(b, h, nb, MOBA_BLOCK, hd)
    vb = v.reshape(b, h, nb, MOBA_BLOCK, hd)
    kmean = jnp.mean(kb, axis=-2)
    nch = sp // QUERY_CHUNK
    qc = jnp.moveaxis(q.reshape(b, h, nch, QUERY_CHUNK, hd), 2, 0)
    starts = jnp.arange(nch, dtype=jnp.int32) * QUERY_CHUNK
    ksel = min(MOBA_TOPK, nb)
    bi = jnp.arange(b)[:, None, None, None]
    hi = jnp.arange(h)[None, :, None, None]
    tabf = tab.astype(jnp.float32)

    def chunk(args):
        qi, start = args
        pos = start + jnp.arange(QUERY_CHUNK, dtype=jnp.int32)
        cur = start // MOBA_BLOCK
        gate = jnp.einsum('bhqd,bhnd->bhqn', qi, kmean).astype(jnp.float32)
        gate = jnp.where(jnp.arange(nb) < cur, gate, NEG_INF_2)
        _, sel = lax.top_k(gate, ksel)
        ks = kb[bi, hi, sel]
        vs = vb[bi, hi, sel]
        s_sel = jnp.einsum('bhqd,bhqnkd->bhqnk', qi, ks).reshape(b, h, QUERY_CHUNK, ksel * MOBA_BLOCK)
        kpos_sel = (sel[..., None] * MOBA_BLOCK + jnp.arange(MOBA_BLOCK)).reshape(b, h, QUERY_CHUNK, ksel * MOBA_BLOCK)
        mask_sel = jnp.repeat(sel < cur, MOBA_BLOCK, axis=-1)
        ko = lax.dynamic_index_in_dim(kb, cur, axis=2, keepdims=False)
        vo = lax.dynamic_index_in_dim(vb, cur, axis=2, keepdims=False)
        s_own = jnp.einsum('bhqd,bhkd->bhqk', qi, ko)
        kpos_own = cur * MOBA_BLOCK + jnp.arange(MOBA_BLOCK, dtype=jnp.int32)
        shp = (b, h, QUERY_CHUNK, MOBA_BLOCK)
        mask_own = jnp.broadcast_to(kpos_own[None, :] <= pos[:, None], shp)
        kpos = jnp.concatenate([kpos_sel, jnp.broadcast_to(kpos_own, shp)], axis=-1)
        mask = jnp.concatenate([mask_sel, mask_own], axis=-1)
        bias = tabf[hi, t5_bucket(pos[:, None] - kpos)]
        sc = jnp.concatenate([s_sel, s_own], axis=-1).astype(jnp.float32) * SCALE + bias
        p, _ = masked_softmax(sc, mask)
        p = p.astype(v.dtype)
        o = (jnp.einsum('bhqnk,bhqnkd->bhqd', p[..., :ksel * MOBA_BLOCK].reshape(b, h, QUERY_CHUNK, ksel, MOBA_BLOCK), vs)
             + jnp.einsum('bhqk,bhkd->bhqd', p[..., ksel * MOBA_BLOCK:], vo))
        return o

    o = lax.map(chunk, (qc, starts))
    return jnp.moveaxis(o, 0, 2).reshape(b, h, sp, hd)[:, :, :s]

def nsa_attention(q, k_cmp, v_cmp, k_slc, v_slc, k_win, v_win, gates, pe_k, pe_v, w1k, w2k, w1v, w2v, tab):
    b, hk, g, s, hd = q.shape
    n_cmp = (s - NSA_CMP_BLOCK) // NSA_CMP_STRIDE + 1
    cidx = np.arange(n_cmp)[:, None] * NSA_CMP_STRIDE + np.arange(NSA_CMP_BLOCK)[None, :]

    def compress(t, pe, w1, w2):
        blk = (t[:, :, cidx] + pe).reshape(b, hk, n_cmp, NSA_CMP_BLOCK * hd)
        return jax.nn.gelu(blk @ w1) @ w2

    kc = compress(k_cmp, pe_k, w1k, w2k)
    vc = compress(v_cmp, pe_v, w1v, w2v)
    pos = np.arange(s)
    mask_c = (np.arange(n_cmp) * NSA_CMP_STRIDE + NSA_CMP_BLOCK - 1)[None, :] <= pos[:, None]
    s_c = jnp.einsum('bhgqd,bhnd->bhgqn', q, kc).astype(jnp.float32) * SCALE
    p_c, _ = masked_softmax(s_c, mask_c)
    o_cmp = jnp.einsum('bhgqn,bhnd->bhgqd', p_c.astype(vc.dtype), vc)
    n_slc = s // NSA_SLC_BLOCK
    c_start = np.arange(n_cmp) * NSA_CMP_STRIDE
    j_start = np.arange(n_slc) * NSA_SLC_BLOCK
    overlap = ((c_start[:, None] < j_start[None, :] + NSA_SLC_BLOCK)
               & (c_start[:, None] + NSA_CMP_BLOCK > j_start[None, :])).astype(np.float32)
    imp = jnp.einsum('bhgqn,nj->bhqj', p_c, jnp.asarray(overlap))
    cur = pos // NSA_SLC_BLOCK
    jj = np.arange(n_slc)[None, :]
    forced = (jj == 0) | (jj == cur[:, None]) | (jj == cur[:, None] - 1)
    imp = jnp.where(forced, -NEG_INF_2, jnp.where(jj <= cur[:, None], imp, NEG_INF_2))
    n_sel = min(NSA_SLC_TOPN, n_slc)
    _, sel = lax.top_k(imp, n_sel)
    ksb = k_slc.reshape(b, hk, n_slc, NSA_SLC_BLOCK, hd)
    vsb = v_slc.reshape(b, hk, n_slc, NSA_SLC_BLOCK, hd)
    nch = s // QUERY_CHUNK
    qc = jnp.moveaxis(q.reshape(b, hk, g, nch, QUERY_CHUNK, hd), 3, 0)
    selc = jnp.moveaxis(sel.reshape(b, hk, nch, QUERY_CHUNK, n_sel), 2, 0)
    starts = jnp.arange(nch, dtype=jnp.int32) * QUERY_CHUNK
    bi = jnp.arange(b)[:, None, None, None]
    hi = jnp.arange(hk)[None, :, None, None]
    tab_t = tab.astype(jnp.float32).transpose(0, 2, 1)

    def chunk(args):
        qi, si, start = args
        pos_q = start + jnp.arange(QUERY_CHUNK, dtype=jnp.int32)
        kk = ksb[bi, hi, si]
        vv = vsb[bi, hi, si]
        nkeys = n_sel * NSA_SLC_BLOCK
        sc = jnp.einsum('bhgqd,bhqnkd->bhgqnk', qi, kk).reshape(b, hk, g, QUERY_CHUNK, nkeys).astype(jnp.float32) * SCALE
        kpos = (si[..., None] * NSA_SLC_BLOCK + jnp.arange(NSA_SLC_BLOCK)).reshape(b, hk, QUERY_CHUNK, nkeys)
        mask = (kpos <= pos_q[:, None])[:, :, None]
        bias = jnp.moveaxis(tab_t[hi, t5_bucket(pos_q[:, None] - kpos)], -1, 2)
        p, _ = masked_softmax(sc + bias, mask)
        return jnp.einsum('bhgqnk,bhqnkd->bhgqd',
                          p.reshape(b, hk, g, QUERY_CHUNK, n_sel, NSA_SLC_BLOCK).astype(vv.dtype), vv)

    o_slc = jnp.moveaxis(lax.map(chunk, (qc, selc, starts)), 0, 3).reshape(b, hk, g, s, hd)
    o_win, _ = banded_attention(q, k_win, v_win, NSA_WINDOW - 1, tab, 1)
    gates = gates.astype(q.dtype)
    return gates[..., 0:1] * o_cmp + gates[..., 1:2] * o_slc + gates[..., 2:3] * o_win

def _heads(t, n):
    b, s, _ = t.shape
    return t.reshape(b, s, n, HEAD_DIM).transpose(0, 2, 1, 3)

def _seq(o):
    b, n, s, d = o.shape
    return o.transpose(0, 2, 1, 3).reshape(b, s, n * d)

def token_mixer(h, w_in_l, rel_bias, sink_l, pe_k, pe_v, w1k, w2k, w1v, w2v, mix_g, w_out_l):
    b, s, _ = h.shape
    H = HEADS_PER_MIXER
    proj = h @ w_in_l
    offs = [int(o) for o in np.cumsum(IN_SIZES)[:-1]]
    (q_a, k_a, v_a, q_b, k_b, v_b, q_c, k_c, v_c,
     q_d, k_dc, v_dc, k_ds, v_ds, k_dw, v_dw, g_d) = jnp.split(proj, offs, axis=-1)
    tabs = [rel_bias[:, i * H:(i + 1) * H].T for i in range(N_MIXERS)]
    o_a = dilated_attention(_heads(q_a, H), _heads(k_a, H), _heads(v_a, H), tabs[0])
    gb = H // SWA_KV_HEADS
    o_b, _ = banded_attention(_heads(q_b, H).reshape(b, SWA_KV_HEADS, gb, s, HEAD_DIM),
                              _heads(k_b, SWA_KV_HEADS), _heads(v_b, SWA_KV_HEADS),
                              SWA_WINDOW - 1, tabs[1].reshape(SWA_KV_HEADS, gb, REL_BUCKETS), 1,
                              sink_l.reshape(SWA_KV_HEADS, gb))
    o_b = o_b.reshape(b, H, s, HEAD_DIM)
    o_c = moba_attention(_heads(q_c, H), _heads(k_c, H), _heads(v_c, H), tabs[2])
    gd = H // NSA_KV_HEADS
    gates = jax.nn.sigmoid(g_d.reshape(b, s, H, 3)).transpose(0, 2, 1, 3).reshape(b, NSA_KV_HEADS, gd, s, 3)
    kvh = lambda t: _heads(t, NSA_KV_HEADS)
    o_d = nsa_attention(_heads(q_d, H).reshape(b, NSA_KV_HEADS, gd, s, HEAD_DIM),
                        kvh(k_dc), kvh(v_dc), kvh(k_ds), kvh(v_ds), kvh(k_dw), kvh(v_dw), gates,
                        pe_k, pe_v, w1k, w2k, w1v, w2v, tabs[3].reshape(NSA_KV_HEADS, gd, REL_BUCKETS))
    o_d = o_d.reshape(b, H, s, HEAD_DIM)
    outs = [rmsnorm_2(_seq(o), mix_g[i]) for i, o in enumerate((o_a, o_b, o_c, o_d))]
    return jnp.concatenate(outs, axis=-1) @ w_out_l

def moe_ffn(h, router_w, router_bias, w_gate, w_up, w_down):
    b, s, d = h.shape
    t = h.reshape(b * s, d)
    aff = jax.nn.sigmoid((t @ router_w).astype(jnp.float32))
    score = aff + router_bias.astype(jnp.float32)
    per_group = N_EXPERTS // N_EXPERT_GROUPS
    group_score = lax.top_k(score.reshape(-1, N_EXPERT_GROUPS, per_group), 2)[0].sum(-1)
    _, gsel = lax.top_k(group_score, TOPK_GROUPS)
    gmask = jnp.any(jnp.arange(N_EXPERT_GROUPS)[None, None, :] == gsel[..., None], axis=1)
    emask = jnp.repeat(gmask, per_group, axis=-1)
    _, esel = lax.top_k(jnp.where(emask, score, NEG_INF_2), TOPK_EXPERTS)
    w = jnp.take_along_axis(aff, esel, axis=-1)
    w = w / jnp.sum(w, axis=-1, keepdims=True)
    combine = jnp.sum((esel[..., None] == jnp.arange(N_EXPERTS)) * w[..., None], axis=1).astype(t.dtype)
    y = jnp.zeros_like(t)
    for e in range(N_EXPERTS):
        he = jax.nn.silu(t @ w_gate[e]) * (t @ w_up[e])
        y = y + combine[:, e:e + 1] * (he @ w_down[e])
    return y.reshape(b, s, d)

def second_inputs(seed: int = 0) -> dict:
    key = jax.random.key(seed)
    ks = jax.random.split(key, 24)
    f32 = jnp.float32

    def nrm(k, shape, sc):
        return jax.random.normal(k, shape, f32) * sc

    D, E, F = D_MODEL, N_EXPERTS, D_EXPERT
    cin = NSA_CMP_BLOCK * HEAD_DIM
    return {
        "x": nrm(ks[0], (BATCH, SEQ, D), 1.0),
        "c": nrm(ks[1], (BATCH, D), 1.0),
        "rel_bias": nrm(ks[2], (REL_BUCKETS, N_HEADS_TOTAL), 0.5),
        "router_w": nrm(ks[3], (D, E), D ** -0.5),
        "router_bias": nrm(ks[4], (E,), 0.01),
        "norm1_g": 1.0 + nrm(ks[5], (DEPTH, D), 0.02),
        "norm2_g": 1.0 + nrm(ks[6], (DEPTH, D), 0.02),
        "ada_w": nrm(ks[7], (DEPTH, D, 6 * D), 0.3 * D ** -0.5),
        "ada_b": nrm(ks[8], (DEPTH, 6 * D), 0.02),
        "w_in": nrm(ks[9], (DEPTH, D, IN_COLS), D ** -0.5),
        "nsa_pe_k": nrm(ks[10], (DEPTH, NSA_CMP_BLOCK, HEAD_DIM), 0.5),
        "nsa_pe_v": nrm(ks[11], (DEPTH, NSA_CMP_BLOCK, HEAD_DIM), 0.5),
        "nsa_cmp_w1_k": nrm(ks[12], (DEPTH, cin, NSA_CMP_HIDDEN), cin ** -0.5),
        "nsa_cmp_w2_k": nrm(ks[13], (DEPTH, NSA_CMP_HIDDEN, HEAD_DIM), NSA_CMP_HIDDEN ** -0.5),
        "nsa_cmp_w1_v": nrm(ks[14], (DEPTH, cin, NSA_CMP_HIDDEN), cin ** -0.5),
        "nsa_cmp_w2_v": nrm(ks[15], (DEPTH, NSA_CMP_HIDDEN, HEAD_DIM), NSA_CMP_HIDDEN ** -0.5),
        "sinks": nrm(ks[16], (DEPTH, HEADS_PER_MIXER), 0.5),
        "mix_norm_g": 1.0 + nrm(ks[17], (DEPTH, N_MIXERS, GROUP_WIDTH), 0.02),
        "w_out": nrm(ks[18], (DEPTH, MIX_WIDTH, D), MIX_WIDTH ** -0.5),
        "exp_w_gate": nrm(ks[19], (DEPTH, E, D, F), D ** -0.5),
        "exp_w_up": nrm(ks[20], (DEPTH, E, D, F), D ** -0.5),
        "exp_w_down": nrm(ks[21], (DEPTH, E, F, D), F ** -0.5),
        "final_g": 1.0 + nrm(ks[22], (D,), 0.02),
    }

def second_block(x, c, rel_bias, router_w, router_bias, norm1_g, norm2_g, ada_w, ada_b, w_in,
              nsa_pe_k, nsa_pe_v, nsa_cmp_w1_k, nsa_cmp_w2_k, nsa_cmp_w1_v, nsa_cmp_w2_v,
              sinks, mix_norm_g, w_out, exp_w_gate, exp_w_up, exp_w_down, final_g):
    c_act = jax.nn.silu(c)
    for l in range(DEPTH):
        mod = c_act @ ada_w[l] + ada_b[l]
        sh1, sc1, g1, sh2, sc2, g2 = jnp.split(mod, 6, axis=-1)
        h = rmsnorm_2(x, norm1_g[l]) * (1.0 + sc1[:, None]) + sh1[:, None]
        x = x + g1[:, None] * token_mixer(h, w_in[l], rel_bias, sinks[l], nsa_pe_k[l], nsa_pe_v[l],
                                          nsa_cmp_w1_k[l], nsa_cmp_w2_k[l], nsa_cmp_w1_v[l], nsa_cmp_w2_v[l],
                                          mix_norm_g[l], w_out[l])
        h = rmsnorm_2(x, norm2_g[l]) * (1.0 + sc2[:, None]) + sh2[:, None]
        x = x + g2[:, None] * moe_ffn(h, router_w, router_bias, exp_w_gate[l], exp_w_up[l], exp_w_down[l])
    return rmsnorm_2(x, final_g)


def setup_inputs(seed=0):
    out = dict(first_inputs(seed))
    for name, value in second_inputs(seed + 1).items():
        if name != "x":
            out[name + "_2"] = value
    return out


def reference(
    x, mem, mix_norm_g, mem_norm_g, w_in, gate_b, conv_w, conv_b, conv_ln_g, conv_ln_b,
    w_conv_out, rel_bias, w_attn_out, w_mem_kv, w_mem_out, w_o, ffn_norm_g, w_up, ffn_conv_w,
    ffn_conv_b, w_down, final_norm_g, c_2, rel_bias_2, router_w_2, router_bias_2, norm1_g_2,
    norm2_g_2, ada_w_2, ada_b_2, w_in_2, nsa_pe_k_2, nsa_pe_v_2, nsa_cmp_w1_k_2, nsa_cmp_w2_k_2,
    nsa_cmp_w1_v_2, nsa_cmp_w2_v_2, sinks_2, mix_norm_g_2, w_out_2, exp_w_gate_2, exp_w_up_2,
    exp_w_down_2, final_g_2,
):
    x = first_block(
        x, mem, mix_norm_g, mem_norm_g, w_in, gate_b, conv_w, conv_b, conv_ln_g, conv_ln_b,
        w_conv_out, rel_bias, w_attn_out, w_mem_kv, w_mem_out, w_o, ffn_norm_g, w_up,
        ffn_conv_w, ffn_conv_b, w_down, final_norm_g,
    )
    return second_block(
        x, c_2, rel_bias_2, router_w_2, router_bias_2, norm1_g_2, norm2_g_2, ada_w_2, ada_b_2,
        w_in_2, nsa_pe_k_2, nsa_pe_v_2, nsa_cmp_w1_k_2, nsa_cmp_w2_k_2, nsa_cmp_w1_v_2,
        nsa_cmp_w2_v_2, sinks_2, mix_norm_g_2, w_out_2, exp_w_gate_2, exp_w_up_2, exp_w_down_2,
        final_g_2,
    )


_drawn_inputs = setup_inputs


def setup_inputs(seed=0):
    import zlib

    import numpy as np

    out = dict(_drawn_inputs(seed))
    spreads = {}
    factors = {'mem_norm_g': 7.987,
     'gate_b': 2.787,
     'conv_b': 2.804,
     'conv_ln_b': 5.496,
     'rel_bias': 4.691,
     'ffn_conv_b': 2.709,
     'norm1_g_2': 8.0,
     'norm2_g_2': 3.362,
     'nsa_pe_k_2': 8.0,
     'nsa_cmp_w1_k_2': 2.932,
     'nsa_cmp_w2_k_2': 2.779,
     'sinks_2': 64.0,
     'mix_norm_g_2': 8.0,
     'final_g_2': 7.968}
    for name, (base, spread) in spreads.items():
        noise = np.random.default_rng([zlib.crc32(name.encode()), seed]).standard_normal(out[name].shape)
        drawn = base * np.exp(spread * noise) if base else spread * noise
        out[name] = __import__('jax').numpy.asarray(drawn.astype(out[name].dtype))
    for name, factor in factors.items():
        out[name] = (out[name] * factor).astype(out[name].dtype)
    return out
```

```python
from contextlib import ExitStack, contextmanager

import numpy as np

import concourse.bass as bass
from concourse import mybir

F32 = mybir.dt.float32
F32R = mybir.dt.float32r
U32 = mybir.dt.uint32
ALU = mybir.AluOpType
ACT = mybir.ActivationFunctionType
AX = mybir.AxisListType

P = 128
S = 256
D = 2048
DC = D // P
HALF = D // 2
HC = HALF // P
TAPS = 31
PAD = TAPS - 1
DFF = 5632
FC = DFF // P
G1 = FC // 4
NE = 16
EPS = 1e-6
NEG = -1e30
NCMP = (S - 32) // 16 + 1
RAW = 2
SPL = 4
AHEAD = SPL - 1
POOLC = 75

PHASES = [("km", HC, "A"), ("vm", HC, "A"), ("qm", HC, "A"), ("q", HC, "A"), ("k", HC, "A"),
          ("v", HC, "A"), ("glu", 2 * HC, "A"), ("gates", 3 * DC, "A"), ("ya", HC, "D"),
          ("ym", HC, "D"), ("yc", HC, "D"), ("wo", DC, "D"), ("ffn", 12 * G1, None),
          ("q2", 16, "A"), ("k2", 12, "A"), ("v2", 8, "A"), ("mixed2", 4, "A"), ("wout", DC, "D"),
          ("moe", 12 * NE, None)]


def owners():
    own = ""
    for _, n, who in PHASES:
        if who:
            own += who * n
        else:
            own += "A" * 8 + "AAAADDDDAAAA" * (n // 12 - 1) + "DDDD"
    return own


OWN = owners()
NT = len(OWN)
BASE = {}
_at = 0
for _name, _n, _ in PHASES:
    BASE[_name] = _at
    _at += _n

PARAMS = [("mem_norm_g", 16), ("mix_norm_g", 16), ("ffn_norm_g", 16), ("final_norm_g", 16),
          ("norm1_g", 16), ("norm2_g", 16), ("mix2_g", 16), ("final2_g", 16), ("gate_b", 48),
          ("conv_b", 8), ("ln_g", 8), ("ln_b", 8), ("ada_b", 96), ("c", 16),
          ("fconv_w", 3 * 88), ("fconv_b", 88), ("conv_w", TAPS * 8)]
PCOL = {}
_at = 0
for _name, _n in PARAMS:
    PCOL[_name] = (_at, _n)
    _at += _n
NPAR = _at


class Tile:

    def __init__(self, k, i=None, n=0, body=None):
        self.k, self.i, self.n, self.body = k, i, n, k if body is None else body

    def __add__(self, m):
        return Tile(self.k + m, self.i, self.n, self.body)

    def plus(self, value, slope):
        return value if self.i is None else value + slope * self.i

    def count(self):
        return self.plus(self.k + 1, self.n)

    def emptied(self, who):
        if self.i is None:
            return OWN[:max(self.k + 1, 0)].count(who)
        each = OWN[self.body:self.body + self.n].count(who)
        if each == 0:
            return OWN[:self.k + 1 + self.n].count(who)
        return OWN[:self.k + 1 + self.n].count(who) - each + each * self.i


class Tally:

    def __init__(self, sem):
        self.sem, self.n, self.i, self.per = sem, 0, None, 0

    def value(self):
        return self.n if self.i is None else self.n + self.per * self.i

    def add(self, ins):
        ins.then_inc(self.sem, 1)
        self.n += 1
        return self.value()

    @contextmanager
    def loop(self, i, per, rounds):
        self.i, self.per, began = i, per, self.n
        yield
        assert self.n - began == per, (self.n - began, per)
        self.i, self.n = None, began + per * rounds


def wait(eng, sem, value):
    if not isinstance(value, int) or value > 0:
        eng.wait_ge(sem, value)


KV_ORDER = [0, 4, 1, 5, 2, 6, 3, 7]
MEM_UNITS = [dict(kind="mem", q=2 * h, k=2 * h, v=2 * h) for h in range(4)]
LOCAL_UNITS = [dict(kind="local", q=h // 2, half=h % 2, k=h // 2, v=h // 2, head=h) for h in range(16)]


def second_units():
    out = []
    for h in range(8):
        out.append(dict(kind="causal", q=h // 2, half=h % 2, k=h // 2, v=h // 2, row=h))
    for h in range(8):
        g = KV_ORDER[h]
        out.append(dict(kind="sink", q=4 + h // 2, half=h % 2, k=8, v=9, row=8 + g, head=g))
    for h in range(8):
        out.append(dict(kind="causal", q=8 + h // 2, half=h % 2, k=4 + h // 2, v=4 + h // 2, row=16 + h))
    for h in range(8):
        g = KV_ORDER[h]
        base = dict(q=12 + h // 2, half=h % 2, row=24 + g)
        out.append(dict(kind="causal", k=10, v=10, gate=3 * g + 1, part=0, **base))
        out.append(dict(kind="causal", k=11, v=11, gate=3 * g + 2, part=1, **base))
        out.append(dict(kind="cmp", k=None, v=None, gate=3 * g, part=2, **base))
    return out


SECOND_UNITS = second_units()
ALL_UNITS = MEM_UNITS + LOCAL_UNITS + SECOND_UNITS


def bias_dmas(unit):
    return {"mem": 0, "cmp": 0, "local": 4}.get(unit["kind"], 2)


def bias_total(u):
    return sum(bias_dmas(x) for x in ALL_UNITS[u % 2:u + 1:2])


NORMS = [("mem", 16), ("x", 16), ("lnmean", 8), ("lnvar", 8), ("ffn", 16), ("final", 16),
         ("norm1", 16), ("mixa", 4), ("mixb", 4), ("mixc", 4), ("mixd", 4), ("norm2", 16), ("final2", 16)]
NORM_AT = {n: k for k, (n, _) in enumerate(NORMS)}
PRE_AT, _at = {}, 0
for _name, _n in NORMS:
    PRE_AT[_name] = _at
    _at += 0 if _name == "lnmean" else _n
SQ_AT, _at = {}, 0
for _name, _n in NORMS:
    SQ_AT[_name] = _at
    _at += 0 if _name == "lnmean" else _n // 4
SPLITS = [("mem", 16), ("x", 16), ("oa", 8), ("om", 8), ("cv", 8), ("merged", 16), ("ffn", 16),
          ("norm1", 16), ("mixa", 4), ("mixb", 4), ("mixc", 4), ("mixd", 4), ("norm2", 16)]
SPLIT_AT, _at = {}, 0
for _name, _n in SPLITS:
    SPLIT_AT[_name] = (_at, _n)
    _at += _n


def split_end(name):
    return sum(SPLIT_AT[name])


ADA_STEPS = {2: 1, 3: 2, 4: 3, 5: 4, 8: 5, 9: 6, 10: 7, 11: 8}


def build(nc, tiles, ada_tiles, x_d, mem_d, params_d, rel_rev, onehot_d, maskrow_d, ident_d,
          cmpmask_d, tab_d, sinks_d, rbias_d, router_d, gd_d, w1_d, w2_d, pe_d, grp_d, out, fbias_d, comb_d):
    with ExitStack() as ctx:
        def sb(name, shape, dt=F32):
            return ctx.enter_context(nc.sbuf_tensor(name, shape, dt))

        def ps(name, shape):
            return ctx.enter_context(nc.psum_tensor(name, shape, F32))

        def sem(name):
            return ctx.enter_context(nc.semaphore(name))

        raw = sb("raw", [P, RAW, 2048])
        w_hi = sb("w_hi", [P, SPL, 2048], F32R)
        w_lo = sb("w_lo", [P, SPL, 2048], F32R)
        a_hi = sb("a_hi", [P, DC, S], F32R)
        a_lo = sb("a_lo", [P, DC, S], F32R)
        h_hi = sb("h_hi", [P, 4, S], F32R)
        h_lo = sb("h_lo", [P, 4, S], F32R)
        pool = sb("pool", [P, POOLC, S])
        par = sb("par", [P, NPAR])
        ones = sb("ones", [P, P])
        ident = sb("ident", [P, P])
        small = sb("small", [P, 704])
        rstd = sb("rstd", [P, S])
        var = sb("var", [P, S])
        mod = sb("mod", [P, 96])
        scale1 = sb("scale1", [P, DC])
        scale2 = sb("scale2", [P, DC])
        cact = sb("cact", [P, DC])
        idx = sb("idx", [P, 8], U32)

        psT = ps("psT", [P, 2, 1024])
        psS = ps("psS", [P, 2, 512])
        psP = ps("psP", [P, 512])
        psO = ps("psO", [P, 512])
        psN = psO[:, 0:S]

        landed = [sem(f"tile_landed{s}") for s in range(RAW)]
        hi_done, lo_done, used = sem("tile_hi_done"), sem("tile_lo_done"), sem("tile_multiplied")
        emptied = {"A": sem("sums_emptied_act"), "D": sem("sums_emptied_dve")}
        L = {n: sem(f"loaded_{n}") for n in
             ("par", "mem", "x", "x_again", "ident", "tables", "sinks", "w1", "cmp", "gd", "router", "comb")}
        names = ["ones_set", "squares_ready", "sums_part", "variance_ready", "std_ready", "normed_ready",
                 "act_hi_ready", "act_lo_ready", "scores_ready", "max_ready", "exp_ready", "recip_ready",
                 "probs_ready", "probs_transposed", "probs_copied", "pv_ready", "head_out", "centered",
                 "conv_in", "conv_done", "dve_step", "merged_ready", "taps_done",
                 "silu_done", "pairs_read", "hidden_hi", "hidden_lo", "ada_used", "ada_summed",
                 "ada_sums", "ada_copied", "bias_rows", "bias_rows_copied",
                 "bias_rows_stored", "gd_hi", "gd_lo", "gd_sums", "gd_ready", "cmp_in", "cmp_hidden",
                 "cmp_gelu", "cmp_tanh", "cmp_out", "cmp_ready", "cv_silu", "router_hi",
                 "router_lo", "router_sums", "affinity", "combine", "combine_tr", "combine_copied",
                 "combine_stored", "y_ready", "output_stored", "final_ready", "masks_set", "c_act",
                 "first_out", "mean_sums", "cmp_sums", "cmp_out_used"]
        W = {n: sem(n) for n in names}
        bias_landed = [sem(f"bias_landed{i}") for i in range(2)]
        ada_landed = [sem(f"ada_landed{i}") for i in range(2)]

        def pc(name, j=None, n=1):
            at, width = PCOL[name]
            if j is None:
                return par[:, at:at + width]
            return par[:, at + j:at + j + n] if isinstance(j, int) else par[:, bass.ds(j + at, n)]

        def chunks(a, n):
            return pool[:, a:a + n, :]

        def flat(a, n):
            return pool[:, a:a + n, :].rearrange("p c s -> p (c s)")

        X, MEMX, KM, VM = 0, 16, 32, 40
        QM, Q, CV = 48, 56, 64
        K, V = 16, 24
        SQ = 64
        SQLN = 48
        GLU = 44
        B0, B1, B2 = 0, 16, 32
        H = 32
        ADA, ADACC = 0, 16
        US, YS, HF = 20, 25, 48
        PRE = 0
        Q2, K2, V2, W1, KP = 0, 16, 48, 64, 30
        SC1, SC2 = 0, 60
        Y, COMB, ES = 0, 16, 52
        GDRAW, RRAW = 60, 60
        slots = flat(CV, 11)[:, 0:(HC + 1) * (S + PAD)].rearrange("p (c s) -> p c s", c=HC + 1)
        hp = slots[:, 1:HC + 1, :]

        cv = slots[:, 0:HC, 0:S]

        def one(name, src, c):
            return cv[:, c, :] if name in ("cv", "lnvar") else pool[:, src + c, :]
        us = flat(US, 5)[:, 0:4 * (S + 2)].rearrange("p (c s) -> p c s", c=4)

        _cols = [0]

        def col(n):
            _cols[0] += n
            return small[:, _cols[0] - n:_cols[0]]

        mx, nmx, den, rden = col(4), col(4), col(4), col(4)
        sinks, esink = col(8), col(4)
        gd = col(48)
        cm_add, cm_mul = col(2 * NCMP), col(2 * NCMP)
        zero = col(1)
        kc_sb = col(NCMP)
        vc_sb = col(P)[0:NCMP, :]
        rb, grp = col(NE), col(NE)
        aff = col(2 * NE)
        w8, m8, gi = col(8), col(8), col(1)
        score, emask, comb = col(NE), col(NE), col(2 * NE)
        iota = col(NE)
        c_x, c_u, c_g = col(2 * NCMP), col(2 * NCMP), col(2 * NCMP)

        def gate_col(part, qt, j):
            return gd[:, 24 * qt + j:24 * qt + j + 1]

        block = ctx.enter_context(nc.Block())

        @block.sync
        def _(sp):
            def load_tile(t):
                wait(sp, lo_done, (t + -RAW).count())
                sp.dma_start(raw[:, t.k % RAW, :], tiles[t.k if t.i is None else t.i * t.n + t.k])\
                    .then_inc(landed[t.k % RAW], 16)

            for k in range(4):
                load_tile(Tile(k))
            with sp.Fori(0, NT // 4 - 1) as i:
                for k in range(4):
                    load_tile(Tile(4 + k, i, 4))
            for g in range(4):
                sp.wait_ge(W["final_ready"], 4 * g + 4)
                sp.dma_start(out[:, 4 * g:4 * g + 4, :], chunks(H + 4 * g, 4)).then_inc(W["output_stored"], 16)
            sp.wait_ge(W["output_stored"], 64)

        @block.scalar
        def _(act):
            def split(t):
                if t.i is None and t.k >= NT:
                    return
                wait(act, used, (t + -SPL).count())
                act.wait_ge(landed[t.k % RAW], t.plus(16 * (t.k // RAW + 1), 16 * (t.n // RAW)))
                nc.scalar.activation(w_hi[:, t.k % SPL, :], raw[:, t.k % RAW, :], ACT.Copy).then_inc(hi_done, 1)

            def sums(t, n=S):
                act.wait_ge(used, t.count())
                return psT[:, t.k % 2, 0:n]

            def linear(name, n, dest, scale):
                peeled = 4 if name == "km" else 0
                for k in range(peeled):
                    split(Tile(k + AHEAD))
                    nc.scalar.activation(pool[:, dest + k, :], sums(Tile(k)), ACT.Copy, scale=scale)\
                        .then_inc(emptied["A"], 1)
                with act.Fori(0, (n - peeled) // 4) as i:
                    for k in range(4):
                        t = Tile(BASE[name] + peeled + k, i, 4)
                        split(t + AHEAD)
                        nc.scalar.activation(pool[:, bass.ds(i * 4 + (dest + peeled + k), 1), :], sums(t), ACT.Copy,
                                             scale=scale).then_inc(emptied["A"], 1)

            def others(name, n):
                with act.Fori(0, n // 4) as i:
                    for k in range(4):
                        split(Tile(BASE[name] + k, i, 4) + AHEAD)

            def norm(name, src, sq=SQ):
                n = dict(NORMS)[name]
                for g in range(n // 4):
                    at = SQ_AT[name] + g
                    wait(act, W["sums_part"], at - 1)
                    nc.scalar.activation(chunks(sq + 4 * (at % 2), 4), (cv[:, 4 * g:4 * g + 4, :] if name == "lnvar" else chunks(src + 4 * g, 4)),
                                         ACT.Square).then_inc(W["squares_ready"], 1)
                act.wait_ge(W["variance_ready"], NORM_AT[name] + 1)
                nc.scalar.activation(var[:, :], var[:, :], ACT.Sqrt).then_inc(W["std_ready"], 1)

            def hi(name, src, dst, bias=None, pre=None):
                for c in range(SPLIT_AT[name][1]):
                    if pre:
                        act.wait_ge(W["normed_ready"], PRE_AT[pre] + c + 1)
                    nc.scalar.activation(a_hi[:, dst + c, :], one(name, src, c), ACT.Identity,
                                         bias=zero if bias is None else bias[:, c:c + 1])\
                        .then_inc(W["act_hi_ready"], 1)

            def attend(units, at, scratch):
                n = len(units)
                for u in range(n + 2):
                    if u < n:
                        unit, slot = units[u], (at + u) % 2
                        act.wait_ge(W["max_ready"], at + u + 1)
                        for qt in range(2):
                            w = {"mem": S, "cmp": NCMP}.get(unit["kind"], S if qt else P)
                            j = 2 * slot + qt
                            dst = pool[:, scratch + j, 0:w]
                            src = psS[:, slot, qt * S:qt * S + w] if unit["kind"] == "mem" else dst
                            kw = {} if unit["kind"] == "cmp" else dict(accum_out=den[:, j:j + 1])
                            last = nc.scalar.activation(dst, src, ACT.Exp, bias=nmx[:, j:j + 1], **kw)
                            if unit["kind"] == "sink":
                                h = unit["head"]
                                last = nc.scalar.activation(esink[:, j:j + 1], nmx[:, j:j + 1], ACT.Exp,
                                                            bias=sinks[:, h:h + 1])
                        last.then_inc(W["exp_ready"], 1)
                    if u >= 2:
                        v = u - 2
                        unit, slot = units[v], (at + v) % 2
                        act.wait_ge(W["probs_transposed"], at + v + 1)
                        wait(act, W["pv_ready"], at + v - 1)
                        dst = flat(scratch + 4 + 2 * slot, 2)
                        if unit["kind"] == "cmp":
                            ins = nc.scalar.activation(dst[0:NCMP, 0:S], psP[0:NCMP, 0:S], ACT.Copy)
                        else:
                            w = 2 * S if unit["kind"] == "mem" else S + P
                            ins = nc.scalar.activation(dst[:, 0:w], psP[:, 0:w], ACT.Copy)
                        ins.then_inc(W["probs_copied"], 1)

            act.dma_start(chunks(MEMX, DC), mem_d).then_inc(L["mem"], 16)
            act.dma_start(par[:, :], params_d).then_inc(L["par"], 16)
            act.dma_start(chunks(X, DC), x_d).then_inc(L["x"], 16)
            act.dma_start(ident[:, :], ident_d).then_inc(L["ident"], 16)

            act.wait_ge(L["mem"], 16)
            act.wait_ge(W["ones_set"], 3)
            norm("mem", MEMX)
            for k in range(AHEAD):
                split(Tile(k))
            hi("mem", MEMX, 0, pre="mem")
            linear("km", HC, KM, 1.0)
            linear("vm", HC, VM, 1.0)
            act.wait_ge(L["x"], 16)
            norm("x", X)
            act.wait_ge(used, BASE["qm"])
            hi("x", X, 0, pre="x")
            linear("qm", HC, QM, 1.0 / 16)
            attend(MEM_UNITS, 0, SC1)
            linear("q", HC, Q, 1.0 / 8)
            linear("k", HC, K, 1.0)
            linear("v", HC, V, 1.0)
            attend(LOCAL_UNITS, 4, SC1)
            with act.Fori(0, HC // 2) as i:
                for k in range(4):
                    t = Tile(BASE["glu"] + k, i, 4)
                    split(t + AHEAD)
                    if k % 2 == 0:
                        act.wait_ge(W["conv_in"], 2 * i + (k // 2 + 1))
                    nc.scalar.activation(pool[:, GLU + k, :], sums(t), ACT.Copy if k % 2 else ACT.Sigmoid)\
                        .then_inc(emptied["A"], 1)
            act.wait_ge(W["head_out"], 20)
            act.wait_ge(W["conv_in"], 2 + HC)
            with act.Fori(0, 4) as i:
                for k in range(12):
                    t = Tile(BASE["gates"] + k, i, 12)
                    split(t + AHEAD)
                    nc.scalar.activation(pool[:, bass.ds(12 * i + k, 1), :], sums(t), ACT.Sigmoid,
                                         bias=pc("gate_b", 12 * i + k)).then_inc(emptied["A"], 1)
            hi("oa", Q, 8)
            hi("om", QM, 0)
            act.wait_ge(W["centered"], 1)
            act.wait_ge(W["act_lo_ready"], split_end("om"))
            norm("lnvar", CV, SQLN)
            others("ya", HC)
            for c in range(HC):
                act.wait_ge(W["normed_ready"], PRE_AT["lnvar"] + c + 1)
                nc.scalar.activation(cv[:, c, :], cv[:, c, :], ACT.Silu,
                                     bias=pc("ln_b", c)).then_inc(W["cv_silu"], 1)
            act.wait_ge(W["cv_silu"], HC)
            act.wait_ge(used, BASE["ym"])
            hi("cv", CV, 8)
            others("ym", HC)
            others("yc", HC)
            act.wait_ge(W["merged_ready"], 2 * HC)
            hi("merged", B1, 0)
            others("wo", DC)
            act.wait_ge(emptied["D"], OWN[:BASE["ffn"]].count("D"))
            norm("ffn", H)
            act.wait_ge(used, BASE["ffn"])
            hi("ffn", PRE, 0, pre="ffn")

            def ffn_up(t, g, half, row):
                for k in range(4):
                    split(t + k + AHEAD)
                    f = 8 * g + (4 * half + k)
                    if k % 2 == 0:
                        act.wait_ge(W["pairs_read"], 4 * g + (2 * half + k // 2 + 1))
                    src = sums(t + k)
                    nc.scalar.activation(us[:, k, 2:2 + S], src, ACT.Copy)
                    nc.scalar.activation(pool[:, YS + k, :], src, ACT.Identity, scale=row("fconv_w", 2 * 88 + f),
                                         bias=row("fconv_b", f)).then_inc(emptied["A"], 1)
                    if k % 2:
                        act.wait_ge(W["taps_done"], 8 * g + (4 * half + k + 1))
                        nc.scalar.activation(pool[:, YS + k, :], pool[:, YS + k, :], ACT.Silu)\
                            .then_inc(W["silu_done"], 1)

            def expert_up(t, g, half, row):
                for k in range(4):
                    split(t + k + AHEAD)
                    if k % 2 == 0:
                        act.wait_ge(W["pairs_read"], 4 * g + (4 * G1 + 2 * half + k // 2 + 1))
                    nc.scalar.activation(pool[:, ES + k, :], sums(t + k), ACT.Copy if k % 2 else ACT.Silu)\
                        .then_inc(emptied["A"], 1)

            def hidden_hi(t, g, before):
                act.wait_ge(W["pairs_read"], 4 * g + (4 * before + 6))
                act.wait_ge(used, t.count())
                nc.scalar.activation(h_hi[:, :, :], chunks(HF, 4), ACT.Copy).then_inc(W["hidden_hi"], 1)

            def groups(name, up, n, before):
                b = BASE[name]
                for half in range(2):
                    up(Tile(b + 4 * half), 0, half, pc)
                hidden_hi(Tile(b + 7), 0, before)
                with act.Fori(0, n - 1) as i:
                    t = Tile(b + 8, i, 12)
                    up(t, i + 1, 0, pc)
                    for k in range(4):
                        split(t + 4 + k + AHEAD)
                    up(t + 8, i + 1, 1, pc)
                    hidden_hi(t + 11, i + 1, before)
                for k in range(4):
                    split(Tile(b + 12 * n - 4 + k) + AHEAD)

            act.wait_ge(L["par"], 16)
            nc.scalar.activation(cact[:, :], pc("c"), ACT.Silu).then_inc(W["c_act"], 1)
            groups("ffn", ffn_up, G1, 0)
            act.wait_ge(emptied["D"], OWN[:BASE["q2"]].count("D"))
            norm("final", H)
            act.wait_ge(W["normed_ready"], PRE_AT["norm1"])
            norm("norm1", H)
            act.wait_ge(used, BASE["q2"])
            hi("norm1", PRE, 0, bias=mod[:, 0:16], pre="norm1")
            linear("q2", 16, Q2, 1.0 / 8)
            linear("k2", 12, K2, 1.0)
            linear("v2", 8, V2, 1.0)
            act.wait_ge(L["gd"], 16)
            hflat = h_hi[:, :, :].rearrange("p c s -> p (c s)")
            nc.scalar.activation(hflat[:, 0:384], flat(GDRAW, 2)[:, 0:384], ACT.Copy).then_inc(W["gd_hi"], 1)
            for k in range(4):
                t = Tile(BASE["mixed2"] + k)
                split(t + AHEAD)
                nc.scalar.activation(pool[:, V2 + 8 + k, :], sums(t), ACT.Copy).then_inc(emptied["A"], 1)
            act.wait_ge(W["gd_sums"], 1)
            nc.scalar.activation(gd, psO[:, 0:48], ACT.Sigmoid).then_inc(W["gd_ready"], 1)
            for r in range(2):
                act.wait_ge(W["cmp_gelu"], 2 * r + 1)
                nc.scalar.activation(c_u, c_u, ACT.Tanh, scale=float(np.sqrt(2 / np.pi)))\
                    .then_inc(W["cmp_tanh"], 1)
            attend(SECOND_UNITS, 20, SC2)
            act.wait_ge(W["head_out"], 52)
            for m in range(4):
                name = "mix" + "abcd"[m]
                norm(name, Q2 + 4 * m)
                hi(name, Q2 + 4 * m, 4 * m, pre=name)
            others("wout", DC)
            act.wait_ge(emptied["D"], OWN[:BASE["moe"]].count("D"))
            norm("norm2", H)
            act.wait_ge(used, BASE["moe"])
            hi("norm2", PRE, 0, bias=mod[:, 48:64], pre="norm2")
            act.wait_ge(L["router"], 16)
            nc.scalar.activation(hflat[:, 0:256], flat(RRAW, 1)[:, 0:256], ACT.Copy).then_inc(W["router_hi"], 1)
            act.wait_ge(W["router_sums"], 1)
            nc.scalar.activation(aff, psO[:, 0:32], ACT.Sigmoid).then_inc(W["affinity"], 1)
            act.wait_ge(W["combine_tr"], 1)
            nc.scalar.activation(pool[0:NE, RRAW + 2, :], psP[0:NE, 0:S], ACT.Copy).then_inc(W["combine_copied"], 1)
            groups("moe", expert_up, NE, G1)
            act.wait_ge(W["first_out"], DC)
            norm("final2", H)

        @block.tensor
        def _(pe):
            def begin(t):
                pe.wait_ge(lo_done, t.count())
                for who in "AD":
                    wait(pe, emptied[who], (t + -2).emptied(who))

            def three(ps_out, w, x_hi, x_lo, k, first, last):
                slot = w.k % SPL
                wh, wl = w_hi[:, slot, k * P:k * P + P], w_lo[:, slot, k * P:k * P + P]
                nc.tensor.matmul(ps_out, wh, x_hi, start=first, stop=False)
                nc.tensor.matmul(ps_out, wh, x_lo, start=False, stop=False)
                return nc.tensor.matmul(ps_out, wl, x_hi, start=False, stop=last)

            def feature_major(t):
                begin(t)
                for k in range(DC):
                    last = three(psT[:, t.k % 2, 0:S], t, a_hi[:, k, :], a_lo[:, k, :], k, k == 0, k == DC - 1)
                last.then_inc(used, 1)

            def token_major(t):
                begin(t)
                slot = t.k % SPL
                for tt in range(2):
                    dst = psT[:, t.k % 2, tt * P:tt * P + P]
                    for k in range(DC):
                        xh, xl = a_hi[:, k, tt * P:tt * P + P], a_lo[:, k, tt * P:tt * P + P]
                        wh, wl = w_hi[:, slot, k * P:k * P + P], w_lo[:, slot, k * P:k * P + P]
                        nc.tensor.matmul(dst, xh, wh, start=k == 0, stop=False)
                        nc.tensor.matmul(dst, xh, wl, start=False, stop=False)
                        last = nc.tensor.matmul(dst, xl, wh, start=False, stop=k == DC - 1)
                last.then_inc(used, 1)

            def half_width(t, a):
                begin(t)
                for n in range(2):
                    for k in range(HC):
                        last = three(psT[:, t.k % 2, n * S:n * S + S], t, a_hi[:, a + k, :], a_lo[:, a + k, :],
                                     HC * n + k, k == 0, k == HC - 1)
                last.then_inc(used, 1)

            def down(t):
                begin(t)
                for n in range(4):
                    for k in range(4):
                        last = three(psT[:, t.k % 2, n * S:n * S + S], t, h_hi[:, k, :], h_lo[:, k, :],
                                     4 * n + k, k == 0, k == 3)
                last.then_inc(used, 1)

            def tiles_of(name, n, multiply, *args):
                peeled = 4 if name in ("km", "ya") else 0
                for k in range(peeled):
                    multiply(Tile(BASE[name] + k), *args)
                with pe.Fori(0, (n - peeled) // 4) as i:
                    for k in range(4):
                        multiply(Tile(BASE[name] + peeled + k, i, 4), *args)

            def norm(name, sq=SQ):
                n = dict(NORMS)[name]
                wait(pe, W["variance_ready"], NORM_AT[name])
                for g in range(n // 4):
                    at = SQ_AT[name] + g
                    pe.wait_ge(W["squares_ready"], at + 1)
                    for c in range(4):
                        last = nc.tensor.matmul(psN, ones[:, :], pool[:, sq + 4 * (at % 2) + c, :],
                                                start=g == 0 and c == 0, stop=g == n // 4 - 1 and c == 3)
                    last.then_inc(W["sums_part"], 1)

            def outs_before(units, u):
                return sum(x.get("part") in (None, 2) for x in units[:u])

            def attend(units, at, scratch, q0, k0, v0, outs):
                n = len(units)
                for u in range(n + 3):
                    if u < n:
                        unit, slot = units[u], (at + u) % 2
                        wait(pe, W["exp_ready"], at + u - 1)
                        for qt in range(2):
                            dst = psS[:, slot, qt * S:qt * S + S]
                            if unit["kind"] == "mem":
                                for c in range(2):
                                    last = nc.tensor.matmul(dst, pool[:, q0 + unit["q"] + c, qt * P:qt * P + P],
                                                            pool[:, k0 + unit["k"] + c, :], start=c == 0, stop=c == 1)
                                continue
                            r = 64 * unit["half"]
                            q = pool[r:r + 64, q0 + unit["q"], qt * P:qt * P + P]
                            if unit["kind"] == "cmp":
                                last = nc.tensor.matmul(dst[:, 0:NCMP], q, kc_sb[r:r + 64, :], start=True, stop=True)
                            else:
                                w = S if qt else P
                                last = nc.tensor.matmul(dst[:, 0:w], q, pool[r:r + 64, k0 + unit["k"], 0:w],
                                                        start=True, stop=True)
                        last.then_inc(W["scores_ready"], 1)
                    if 2 <= u < n + 2:
                        v = u - 2
                        unit, slot = units[v], (at + v) % 2
                        pe.wait_ge(W["probs_ready"], at + v + 1)
                        wait(pe, W["probs_copied"], at + v)
                        for qt in range(2):
                            p = pool[:, scratch + 2 * slot + qt, :]
                            if unit["kind"] == "cmp":
                                last = nc.tensor.transpose(psP[0:NCMP, qt * P:qt * P + P], p[:, 0:NCMP], ident[:, :])
                                continue
                            last = nc.tensor.transpose(psP[:, qt * P:qt * P + P], p[:, 0:P], ident[:, :])
                            if unit["kind"] == "mem":
                                last = nc.tensor.transpose(psP[:, S + qt * P:S + qt * P + P], p[:, P:S], ident[:, :])
                            elif qt:
                                last = nc.tensor.transpose(psP[:, S:S + P], p[:, P:S], ident[:, :])
                        last.then_inc(W["probs_transposed"], 1)
                    if u >= 3:
                        v = u - 3
                        unit, slot = units[v], (at + v) % 2
                        pe.wait_ge(W["probs_copied"], at + v + 1)
                        part = unit.get("part")
                        if part in (None, 0):
                            wait(pe, W["head_out"], outs + outs_before(units, v))
                        pT = flat(scratch + 4 + 2 * slot, 2)
                        if unit["kind"] == "mem":
                            for c in range(2):
                                for kt in range(2):
                                    last = nc.tensor.matmul(psO[:, c * S:c * S + S],
                                                            pool[:, v0 + unit["v"] + c, kt * P:kt * P + P],
                                                            pT[:, kt * S:kt * S + S], start=kt == 0, stop=kt == 1)
                        elif unit["kind"] == "cmp":
                            last = nc.tensor.matmul(psO[:, 0:S], vc_sb, pT[0:NCMP, 0:S], start=False, stop=True)
                        else:
                            vv = pool[:, v0 + unit["v"], :]
                            nc.tensor.matmul(psO[:, 0:S], vv[:, 0:P], pT[:, 0:S], start=part in (None, 0), stop=False)
                            last = nc.tensor.matmul(psO[:, P:S], vv[:, P:S], pT[:, S:S + P], start=False,
                                                    stop=part is None)
                        last.then_inc(W["pv_ready"], 1)

            pe.wait_ge(W["ones_set"], 3)
            norm("mem")
            pe.wait_ge(W["act_lo_ready"], split_end("mem"))
            tiles_of("km", HC, feature_major)
            tiles_of("vm", HC, token_major)
            norm("x")
            pe.wait_ge(W["act_lo_ready"], split_end("x"))
            tiles_of("qm", HC, feature_major)
            pe.wait_ge(L["ident"], 16)
            pe.wait_ge(emptied["A"], BASE["q"])
            pe.wait_ge(W["variance_ready"], 2)
            attend(MEM_UNITS, 0, SC1, QM, KM, VM, 0)
            tiles_of("q", HC, feature_major)
            tiles_of("k", HC, feature_major)
            tiles_of("v", HC, token_major)
            pe.wait_ge(emptied["A"], BASE["glu"])
            attend(LOCAL_UNITS, 4, SC1, Q, K, V, 4)
            tiles_of("glu", 2 * HC, feature_major)
            tiles_of("gates", 3 * DC, feature_major)
            pe.wait_ge(W["conv_done"], HC)
            pe.wait_ge(W["head_out"], 20)
            for c in range(HC):
                last = nc.tensor.matmul(psN, ones[:, :], cv[:, c, :], start=c == 0, stop=c == HC - 1)
            last.then_inc(W["mean_sums"], 1)
            norm("lnvar", SQLN)
            pe.wait_ge(W["act_lo_ready"], split_end("oa"))
            tiles_of("ya", HC, half_width, 8)
            pe.wait_ge(W["act_lo_ready"], split_end("om"))
            tiles_of("ym", HC, half_width, 0)
            pe.wait_ge(W["act_lo_ready"], split_end("cv"))
            tiles_of("yc", HC, half_width, 8)
            pe.wait_ge(W["act_lo_ready"], split_end("merged"))
            tiles_of("wo", DC, feature_major)
            norm("ffn")
            pe.wait_ge(W["act_lo_ready"], split_end("ffn"))

            def ada_reduce(g):
                pe.wait_ge(W["ada_used"], 8 * g + 8)
                for m in range(8):
                    last = nc.tensor.matmul(psP[:, m:m + 1], flat(ADACC, 4)[:, m * P:m * P + P], ones[:, 0:1],
                                            start=True, stop=True)
                last.then_inc(W["ada_sums"], 1)

            def groups(name, n, before, ada):
                b = BASE[name]
                for k in range(8):
                    feature_major(Tile(b + k))
                with pe.Fori(0, n - 1) as i:
                    t = Tile(b + 8, i, 12)
                    for k in range(4):
                        feature_major(t + k)
                        if ada and k == 0:
                            ada_reduce(i)
                    pe.wait_ge(W["hidden_lo"], i + (before + 1))
                    for k in range(4):
                        down(t + 4 + k)
                    for k in range(4):
                        feature_major(t + 8 + k)
                if ada:
                    ada_reduce(n - 1)
                pe.wait_ge(W["hidden_lo"], before + n)
                for k in range(4):
                    down(Tile(b + 12 * n - 4 + k))
                if ada:
                    ada_reduce(n)

            groups("ffn", G1, 0, True)
            pe.wait_ge(L["tables"], 48)
            pe.wait_ge(W["ada_copied"], G1 + 1)
            nc.tensor.matmul(psP[0:32, :], flat(Q2, 1)[0:32, 0:32], flat(Q2 + 1, 2)[0:32, :], start=True, stop=True)\
                .then_inc(W["bias_rows"], 1)
            norm("final")
            norm("norm1")
            pe.wait_ge(W["act_lo_ready"], split_end("norm1"))
            tiles_of("q2", 16, feature_major)
            tiles_of("k2", 12, feature_major)
            tiles_of("v2", 8, token_major)
            feature_major(Tile(BASE["mixed2"]))
            for k in range(1, 4):
                token_major(Tile(BASE["mixed2"] + k))
            pe.wait_ge(W["gd_lo"], 1)
            hh = h_hi[:, :, :].rearrange("p c s -> p (c s)")
            hl = h_lo[:, :, :].rearrange("p c s -> p (c s)")

            def narrow(n):
                for tt in range(2):
                    for k in range(DC):
                        xh, xl = a_hi[:, k, tt * P:tt * P + P], a_lo[:, k, tt * P:tt * P + P]
                        dst = psO[:, tt * n:tt * n + n]
                        nc.tensor.matmul(dst, xh, hh[:, k * n:k * n + n], start=k == 0, stop=False)
                        nc.tensor.matmul(dst, xh, hl[:, k * n:k * n + n], start=False, stop=False)
                        last = nc.tensor.matmul(dst, xl, hh[:, k * n:k * n + n], start=False, stop=k == DC - 1)
                return last

            pe.wait_ge(W["variance_ready"], NORM_AT["norm1"] + 1)
            narrow(24).then_inc(W["gd_sums"], 1)
            for r in range(2):
                pe.wait_ge(W["cmp_in"], r + 1)
                wait(pe, W["cmp_sums"], r)
                for part in range(2):
                    pe.wait_ge(L["w1"], 32 * (2 * r + part + 1))
                    for j in range(2):
                        for i in range(16):
                            last = nc.tensor.matmul(psS[:, j, 0:NCMP], flat(W1, 8)[64 * j:64 * j + 64, i * P:i * P + P],
                                                    flat(KP, 2)[64 * j:64 * j + 64,
                                                                (16 * part + i) * NCMP:(16 * part + i + 1) * NCMP],
                                                    start=part == 0 and i == 0, stop=part == 1 and i == 15)
                    last.then_inc(W["cmp_hidden"], 1)
                pe.wait_ge(W["cmp_gelu"], 2 * r + 2)
                if r == 0:
                    nc.tensor.matmul(psP[:, 0:2 * NCMP], flat(28, 1)[:, 0:P], c_g, start=True, stop=True)\
                        .then_inc(W["cmp_out"], 1)
                else:
                    pe.wait_ge(W["cmp_ready"], 1)
                    for j in range(2):
                        last = nc.tensor.matmul(psP[0:NCMP, 64 * j:64 * j + 64], c_g[:, NCMP * j:NCMP * j + NCMP],
                                                flat(28, 1)[:, P:P + 64], start=True, stop=True)
                    last.then_inc(W["cmp_out"], 1)
            pe.wait_ge(W["gd_ready"], 1)
            pe.wait_ge(W["cmp_ready"], 2)
            pe.wait_ge(emptied["A"], OWN[:BASE["wout"]].count("A"))
            attend(SECOND_UNITS, 20, SC2, Q2, K2, V2, 20)
            for m in range(4):
                if m == 0:
                    pe.wait_ge(W["head_out"], 52)
                norm("mix" + "abcd"[m])
            pe.wait_ge(W["act_lo_ready"], split_end("mixd"))
            tiles_of("wout", DC, feature_major)
            norm("norm2")
            pe.wait_ge(W["act_lo_ready"], split_end("norm2"))
            pe.wait_ge(W["router_lo"], 1)
            pe.wait_ge(W["variance_ready"], NORM_AT["norm2"] + 1)
            narrow(NE).then_inc(W["router_sums"], 1)
            pe.wait_ge(W["combine"], 1)
            for tt in range(2):
                last = nc.tensor.transpose(psP[0:NE, tt * P:tt * P + P], comb[:, tt * NE:tt * NE + NE], ident[:, :])
            last.then_inc(W["combine_tr"], 1)
            groups("moe", NE, G1, False)
            pe.wait_ge(W["affinity"], 1)
            norm("final2")

        @block.vector
        def _(dve):
            step = Tally(W["dve_step"])

            def link(ins):
                dve.wait_ge(step.sem, step.add(ins))

            def lo(t):
                if t.i is None and t.k >= NT:
                    return
                dve.wait_ge(hi_done, t.count())
                nc.vector.tensor_tensor(w_lo[:, t.k % SPL, :], raw[:, t.k % RAW, :],
                                        w_hi[:, t.k % SPL, :].bitcast(F32), ALU.subtract).then_inc(lo_done, 1)

            def others(name, n):
                with dve.Fori(0, n // 4) as i:
                    for k in range(4):
                        lo(Tile(BASE[name] + k, i, 4) + AHEAD)

            def root(name, width):
                m = NORM_AT[name]
                dve.wait_ge(W["sums_part"], SQ_AT[name] + dict(NORMS)[name] // 4)
                nc.vector.tensor_scalar(var[:, :], psN, 1.0 / width, EPS, ALU.mult, ALU.add)\
                    .then_inc(W["variance_ready"], 1)
                dve.wait_ge(W["std_ready"], m + (1 if m < NORM_AT["lnmean"] else 0))
                link(nc.vector.reciprocal(rstd[:, :], var[:, :]))

            def normed(name, src, dst, gain):
                for c in range(dict(NORMS)[name]):
                    nc.vector.scalar_tensor_tensor(one(name, dst, c), one(name, src, c), gain[:, c:c + 1],
                                                   rstd[:, :], ALU.mult, ALU.mult).then_inc(W["normed_ready"], 1)

            def act_lo(name, src, dst, bias=None):
                for c in range(SPLIT_AT[name][1]):
                    dve.wait_ge(W["act_hi_ready"], SPLIT_AT[name][0] + c + 1)
                    nc.vector.scalar_tensor_tensor(a_lo[:, dst + c, :], one(name, src, c),
                                                   zero if bias is None else bias[:, c:c + 1],
                                                   a_hi[:, dst + c, :].bitcast(F32), ALU.add, ALU.subtract)\
                        .then_inc(W["act_lo_ready"], 1)

            def attend(units, at, scratch, q0):
                n = len(units)
                for u in range(n + 3):
                    if u < n:
                        unit, slot = units[u], (at + u) % 2
                        dve.wait_ge(W["scores_ready"], at + u + 1)
                        wait(dve, W["probs_transposed"], at + u - 1)
                        if bias_dmas(unit):
                            dve.wait_ge(bias_landed[slot], 16 * bias_total(at + u))
                        for qt in range(2):
                            w = {"mem": S, "cmp": NCMP}.get(unit["kind"], S if qt else P)
                            j = 2 * slot + qt
                            src = psS[:, slot, qt * S:qt * S + w]
                            if unit["kind"] == "mem":
                                link(nc.vector.reduce_max(mx[:, j:j + 1], src, AX.X))
                            else:
                                add = cm_add[:, qt * NCMP:qt * NCMP + NCMP] if unit["kind"] == "cmp" else \
                                    pool[:, scratch + 8 + j, 0:w]
                                link(nc.vector.tensor_tensor_reduce(
                                    out=pool[:, scratch + j, 0:w], in0=src, in1=add, scale=1.0, scalar=-3.0e38,
                                    op0=ALU.add, op1=ALU.max, accum_out=mx[:, j:j + 1]))
                        if unit["kind"] == "sink":
                            h = unit["head"]
                            for qt in range(2):
                                j = 2 * slot + qt
                                ins = nc.vector.tensor_tensor(mx[:, j:j + 1], mx[:, j:j + 1], sinks[:, h:h + 1], ALU.max)
                            link(ins)
                        nc.vector.tensor_scalar(nmx[:, 2 * slot:2 * slot + 2], mx[:, 2 * slot:2 * slot + 2], -1.0, None,
                                                ALU.mult).then_inc(W["max_ready"], 1)
                    if 1 <= u < n + 1:
                        v = u - 1
                        unit, slot = units[v], (at + v) % 2
                        j = 2 * slot
                        dve.wait_ge(W["exp_ready"], at + v + 1)
                        if unit["kind"] == "cmp":
                            for qt in range(2):
                                e = pool[:, scratch + j + qt, 0:NCMP]
                                link(nc.vector.tensor_tensor_reduce(
                                    out=e, in0=e, in1=cm_mul[:, qt * NCMP:qt * NCMP + NCMP], scale=1.0, scalar=0.0,
                                    op0=ALU.mult, op1=ALU.add, accum_out=den[:, j + qt:j + qt + 1]))
                            link(nc.vector.tensor_scalar(den[:, j:j + 2], den[:, j:j + 2],
                                                         float(np.finfo(np.float32).tiny), None, ALU.max))
                        if unit["kind"] == "sink":
                            link(nc.vector.tensor_tensor(den[:, j:j + 2], den[:, j:j + 2], esink[:, j:j + 2], ALU.add))
                        ins = nc.vector.reciprocal(rden[:, j:j + 2], den[:, j:j + 2])
                        if "gate" in unit:
                            link(ins)
                            for qt in range(2):
                                g = 24 * qt + unit["gate"]
                                ins = nc.vector.tensor_tensor(rden[:, j + qt:j + qt + 1], rden[:, j + qt:j + qt + 1],
                                                              gd[:, g:g + 1], ALU.mult)
                        ins.then_inc(W["recip_ready"], 1)
                    if u >= 3:
                        v = u - 3
                        unit = units[v]
                        if unit.get("part") in (None, 2):
                            dve.wait_ge(W["pv_ready"], at + v + 1)
                            if unit["kind"] == "mem":
                                ins = nc.vector.tensor_copy(chunks(q0 + unit["q"], 2).rearrange("p c s -> p (c s)"),
                                                            psO[:, :])
                            else:
                                r = 64 * unit["half"]
                                ins = nc.vector.tensor_copy(pool[r:r + 64, q0 + unit["q"], :], psO[r:r + 64, 0:S])
                            ins.then_inc(W["head_out"], 1)

            nc.vector.memset(ones[:, :], 1.0).then_inc(W["ones_set"], 1)
            nc.vector.memset(zero, 0.0).then_inc(W["ones_set"], 1)
            nc.vector.memset(w8, -3.0e38).then_inc(W["ones_set"], 1)
            dve.wait_ge(W["ones_set"], 3)

            dve.wait_ge(L["par"], 16)
            root("mem", D)
            normed("mem", MEMX, MEMX, pc("mem_norm_g"))
            for k in range(AHEAD):
                lo(Tile(k))
            act_lo("mem", MEMX, 0)
            others("km", HC)
            others("vm", HC)
            root("x", D)
            normed("x", X, X, pc("mix_norm_g"))
            act_lo("x", X, 0)
            others("qm", HC)
            attend(MEM_UNITS, 0, SC1, QM)
            others("q", HC)
            others("k", HC)
            others("v", HC)
            attend(LOCAL_UNITS, 4, SC1, Q)
            nc.vector.memset(hp[:, :, 0:PAD], 0.0).then_inc(W["conv_in"], 2)
            with dve.Fori(0, HC // 2) as i:
                for k in range(4):
                    t = Tile(BASE["glu"] + k, i, 4)
                    lo(t + AHEAD)
                    if k % 2:
                        dve.wait_ge(emptied["A"], t.emptied("A"))
                        nc.vector.tensor_tensor(hp[:, bass.ds(2 * i + k // 2, 1), PAD:PAD + S], pool[:, GLU + k - 1, :],
                                                pool[:, GLU + k, :], ALU.mult).then_inc(W["conv_in"], 1)
            dve.wait_ge(W["conv_in"], 2 + HC)
            taps = [(j, tap) for j in range(2) for tap in range(TAPS)]
            with dve.Fori(0, 4) as i:
                with step.loop(i, 2 * TAPS - 2, 4):
                    for k in range(12):
                        lo(Tile(BASE["gates"] + k, i, 12) + AHEAD)
                        for j, tap in taps[len(taps) * k // 12:len(taps) * (k + 1) // 12]:
                            c = 2 * i + j
                            dst = cv[:, bass.ds(c, 1), :]
                            src = hp[:, bass.ds(c, 1), tap:tap + S]
                            w = pc("conv_w", 8 * tap + c)
                            if tap == 0:
                                if j:
                                    dve.wait_ge(W["conv_done"], c)
                                link(nc.vector.tensor_scalar(dst, src, w, pc("conv_b", c), ALU.mult, ALU.add))
                                continue
                            ins = nc.vector.scalar_tensor_tensor(dst, src, w, dst, ALU.mult, ALU.add)
                            if tap == TAPS - 1:
                                ins.then_inc(W["conv_done"], 1)
                                if j:
                                    dve.wait_ge(W["conv_done"], c + 1)
                            else:
                                link(ins)
            act_lo("oa", Q, 8)
            act_lo("om", QM, 0)
            dve.wait_ge(W["mean_sums"], 1)
            nc.vector.tensor_scalar(rstd[:, :], psN, 1.0 / HALF, None, ALU.mult).then_inc(W["variance_ready"], 1)
            dve.wait_ge(W["variance_ready"], NORM_AT["lnmean"] + 1)
            for c in range(HC):
                ins = nc.vector.tensor_tensor(cv[:, c, :], cv[:, c, :], rstd[:, :], ALU.subtract)
            ins.then_inc(W["centered"], 1)
            dve.wait_ge(W["centered"], 1)
            root("lnvar", HALF)
            normed("lnvar", CV, CV, pc("ln_g"))

            def gated(name, gates, into):
                with dve.Fori(0, HC // 4) as i:
                    for k in range(4):
                        t = Tile(BASE[name] + k, i, 4)
                        lo(t + AHEAD)
                        dve.wait_ge(used, t.count())
                        g = pool[:, bass.ds(8 * i + (gates + 2 * k), 2), :].rearrange("p c s -> p (c s)")
                        nc.vector.tensor_tensor(g, psT[:, t.k % 2, 0:2 * S], g, ALU.mult).then_inc(emptied["D"], 1)
                        if into is not None:
                            m = pool[:, bass.ds(8 * i + (into + 2 * k), 2), :].rearrange("p c s -> p (c s)")
                            dve.wait_ge(emptied["D"], t.emptied("D"))
                            nc.vector.tensor_tensor(m, m, g, ALU.add).then_inc(W["merged_ready"], 1)

            gated("ya", B1, None)
            dve.wait_ge(emptied["D"], HC)
            act_lo("cv", CV, 8)
            gated("ym", B2, B1)
            dve.wait_ge(W["merged_ready"], HC)
            gated("yc", B0, B1)
            dve.wait_ge(W["merged_ready"], 2 * HC)
            act_lo("merged", B1, 0)
            dve.wait_ge(L["x_again"], 16)
            with dve.Fori(0, DC // 4) as i:
                for k in range(4):
                    t = Tile(BASE["wo"] + k, i, 4)
                    lo(t + AHEAD)
                    dve.wait_ge(used, t.count())
                    h = pool[:, bass.ds(4 * i + (H + k), 1), :]
                    nc.vector.tensor_tensor(h, psT[:, t.k % 2, 0:S], h, ALU.add).then_inc(emptied["D"], 1)
            dve.wait_ge(emptied["D"], OWN[:BASE["ffn"]].count("D"))
            root("ffn", D)
            normed("ffn", H, PRE, pc("ffn_norm_g"))
            act_lo("ffn", PRE, 0)
            nc.vector.memset(us[:, :, 0:2], 0.0).then_inc(W["pairs_read"], 2)

            def ada_tile(j, g):
                acc, src = flat(ADACC, 4), flat(ADA + 8 * (j % 2), 8)
                dve.wait_ge(ada_landed[j % 2], 64 * g + 16 * (j // 2 + 1))
                for r in range(2):
                    c, s = cact[:, 2 * j + r:2 * j + r + 1], src[:, 1024 * r:1024 * r + 1024]
                    if j == 0 and r == 0:
                        ins = nc.vector.tensor_scalar(acc, s, c, None, ALU.mult)
                    else:
                        ins = nc.vector.scalar_tensor_tensor(acc, s, c, acc, ALU.mult, ALU.add)
                    if r == 0:
                        link(ins)
                ins.then_inc(W["ada_used"], 1)
                dve.wait_ge(W["ada_used"], 8 * g + (j + 1))

            def ada_copy(g):
                dve.wait_ge(W["ada_sums"], g + 1)
                dst = mod[:, 8 * g:8 * g + 8] if isinstance(g, int) else mod[:, bass.ds(8 * g, 8)]
                nc.vector.tensor_copy(dst, psP[:, 0:8]).then_inc(W["ada_copied"], 1)

            def ffn_up(t, k, g, half):
                f = 8 * g + (4 * half + k)
                dve.wait_ge(emptied["A"], (t + k).emptied("A"))
                y = pool[:, YS + k, :]
                link(nc.vector.scalar_tensor_tensor(y, us[:, k, 1:1 + S], pc("fconv_w", 88 + f), y, ALU.mult, ALU.add))
                nc.vector.scalar_tensor_tensor(y, us[:, k, 0:S], pc("fconv_w", f), y, ALU.mult, ALU.add)\
                    .then_inc(W["taps_done"], 1)
                if k % 2:
                    dve.wait_ge(W["silu_done"], 4 * g + (2 * half + k // 2 + 1))
                    nc.vector.tensor_tensor(pool[:, HF + 2 * half + k // 2, :], y, pool[:, YS + k - 1, :], ALU.mult)\
                        .then_inc(W["pairs_read"], 1)

            def expert_up(t, k, g, half):
                if k % 2:
                    dve.wait_ge(emptied["A"], (t + k).emptied("A"))
                    h = pool[:, HF + 2 * half + k // 2, :]
                    w = pool[:, COMB + g, :] if isinstance(g, int) else pool[:, bass.ds(g + COMB, 1), :]
                    link(nc.vector.tensor_tensor(h, pool[:, ES + k - 1, :], pool[:, ES + k, :], ALU.mult))
                    nc.vector.tensor_tensor(h, h, w, ALU.mult).then_inc(W["pairs_read"], 1)

            def add_down(t, k, acc):
                dve.wait_ge(used, (t + k).count())
                a = flat(acc + 4 * k, 4)
                nc.vector.tensor_tensor(a, psT[:, (t + k).k % 2, :], a, ALU.add).then_inc(emptied["D"], 1)

            def hidden_lo(g):
                dve.wait_ge(W["hidden_hi"], g + 1)
                nc.vector.tensor_tensor(h_lo[:, :, :], chunks(HF, 4), h_hi[:, :, :].bitcast(F32), ALU.subtract)\
                    .then_inc(W["hidden_lo"], 1)
                dve.wait_ge(W["hidden_lo"], g + 1)

            def groups(name, up, n, before, acc, ada, links):
                b = BASE[name]
                for k in range(8):
                    lo(Tile(b + k) + AHEAD)
                    up(Tile(b + 4 * (k // 4)), k % 4, 0, k // 4)
                    if ada:
                        ada_tile(k, 0)
                hidden_lo(before)
                with dve.Fori(0, n - 1) as i:
                    with step.loop(i, links, n - 1):
                        t = Tile(b + 8, i, 12)
                        for k in range(12):
                            lo(t + k + AHEAD)
                            if 4 <= k < 8:
                                add_down(t + 4, k - 4, acc)
                            else:
                                up(t + 4 * (k // 4), k % 4, i + 1, k // 8)
                            if ada and k == 1:
                                ada_copy(i)
                            if ada and k in ADA_STEPS:
                                ada_tile(ADA_STEPS[k] - 1, i + 1)
                        hidden_lo(i + (before + 1))
                if ada:
                    ada_copy(n - 1)
                for k in range(4):
                    lo(Tile(b + 12 * n - 4 + k) + AHEAD)
                    add_down(Tile(b + 12 * n - 4), k, acc)
                    if ada:
                        for j in (2 * k, 2 * k + 1):
                            ada_tile(j, n)
                if ada:
                    ada_copy(n)

            dve.wait_ge(W["c_act"], 1)
            groups("ffn", ffn_up, G1, 0, H, True, 8 + 8)
            dve.wait_ge(W["ada_copied"], G1 + 1)
            link(nc.vector.tensor_tensor(mod[:, :], mod[:, :], pc("ada_b"), ALU.add))
            nc.vector.scalar_tensor_tensor(scale1[:, :], mod[:, 16:32], 1.0, pc("norm1_g"), ALU.add, ALU.mult)
            link(nc.vector.scalar_tensor_tensor(scale2[:, :], mod[:, 64:80], 1.0, pc("norm2_g"), ALU.add, ALU.mult))
            dve.wait_ge(W["bias_rows"], 1)
            nc.vector.tensor_tensor(flat(Q2 + 5, 2)[0:32, :], psP[0:32, :], flat(Q2 + 3, 2)[0:32, :], ALU.add)\
                .then_inc(W["bias_rows_copied"], 1)
            dve.wait_ge(emptied["D"], OWN[:BASE["q2"]].count("D"))
            root("final", D)
            normed("final", H, H, pc("final_norm_g"))
            root("norm1", D)
            dve.wait_ge(W["bias_rows_stored"], 16)
            normed("norm1", H, PRE, scale1)
            act_lo("norm1", PRE, 0, bias=mod[:, 0:16])
            others("q2", 16)
            others("k2", 12)
            others("v2", 8)
            dve.wait_ge(W["gd_hi"], 1)
            hl = h_lo[:, :, :].rearrange("p c s -> p (c s)")
            hh = h_hi[:, :, :].rearrange("p c s -> p (c s)").bitcast(F32)
            nc.vector.tensor_tensor(hl[:, 0:384], flat(GDRAW, 2)[:, 0:384], hh[:, 0:384], ALU.subtract)\
                .then_inc(W["gd_lo"], 1)
            for k in range(4):
                lo(Tile(BASE["mixed2"] + k) + AHEAD)
            dve.wait_ge(L["cmp"], 80)
            dve.wait_ge(emptied["A"], OWN[:BASE["mixed2"] + 1].count("A"))
            for r in range(2):
                wait(dve, W["cmp_hidden"], 2 * r)
                src = pool[:, V2 + 8 if r else K2 + 9, :].rearrange("p (m b) -> p b m", b=16)
                pe_r = flat(29, 1)[:, 32 * r:32 * r + 32]
                for a in range(2):
                    ins = nc.vector.tensor_tensor(
                        flat(KP, 2)[:, 16 * a * NCMP:16 * (a + 1) * NCMP].rearrange("p (b m) -> p b m", b=16),
                        src[:, :, a:a + NCMP], pe_r[:, 16 * a:16 * a + 16].unsqueeze(2).to_broadcast([P, 16, NCMP]),
                        ALU.add)
                ins.then_inc(W["cmp_in"], 1)
                dve.wait_ge(W["cmp_hidden"], 2 * r + 2)
                for j in range(2):
                    ins = nc.vector.tensor_copy(c_x[:, NCMP * j:NCMP * j + NCMP], psS[:, j, 0:NCMP])
                ins.then_inc(W["cmp_sums"], 1)
                dve.wait_ge(W["cmp_sums"], r + 1)
                link(nc.vector.tensor_tensor(c_u, c_x, c_x, ALU.mult))
                link(nc.vector.tensor_scalar(c_u, c_u, 0.044715, 1.0, ALU.mult, ALU.add))
                nc.vector.tensor_tensor(c_u, c_u, c_x, ALU.mult).then_inc(W["cmp_gelu"], 1)
                dve.wait_ge(W["cmp_tanh"], r + 1)
                link(nc.vector.scalar_tensor_tensor(c_g, c_u, 1.0, c_x, ALU.add, ALU.mult))
                nc.vector.tensor_scalar(c_g, c_g, 0.5, None, ALU.mult).then_inc(W["cmp_gelu"], 1)
                dve.wait_ge(W["cmp_out"], r + 1)
                if r == 0:
                    for j in range(2):
                        ins = nc.vector.tensor_copy(kc_sb[64 * j:64 * j + 64, :],
                                                    psP[64 * j:64 * j + 64, NCMP * j:NCMP * j + NCMP])
                else:
                    ins = nc.vector.tensor_copy(vc_sb, psP[0:NCMP, 0:P])
                ins.then_inc(W["cmp_ready"], 1)
            dve.wait_ge(L["sinks"], 16 * SMALL_LOADS)
            dve.wait_ge(W["gd_ready"], 1)
            attend(SECOND_UNITS, 20, SC2, Q2)
            dve.wait_ge(W["head_out"], 52)
            for m in range(4):
                name = "mix" + "abcd"[m]
                root(name, HALF // 2)
                normed(name, Q2 + 4 * m, Q2 + 4 * m, pc("mix2_g", 4 * m, 4))
                act_lo(name, Q2 + 4 * m, 4 * m)
            with dve.Fori(0, DC // 4) as i:
                for k in range(4):
                    t = Tile(BASE["wout"] + k, i, 4)
                    lo(t + AHEAD)
                    dve.wait_ge(used, t.count())
                    h = pool[:, bass.ds(4 * i + (H + k), 1), :]
                    nc.vector.scalar_tensor_tensor(h, psT[:, t.k % 2, 0:S], mod[:, bass.ds(4 * i + (32 + k), 1)], h,
                                                   ALU.mult, ALU.add).then_inc(emptied["D"], 1)
            dve.wait_ge(emptied["D"], OWN[:BASE["moe"]].count("D"))
            root("norm2", D)
            normed("norm2", H, PRE, scale2)
            act_lo("norm2", PRE, 0, bias=mod[:, 48:64])
            dve.wait_ge(W["router_hi"], 1)
            nc.vector.tensor_tensor(hl[:, 0:256], flat(RRAW, 1)[:, 0:256], hh[:, 0:256], ALU.subtract)\
                .then_inc(W["router_lo"], 1)
            dve.wait_ge(W["affinity"], 1)
            for tt in range(2):
                af, cb = aff[:, NE * tt:NE * tt + NE], comb[:, NE * tt:NE * tt + NE]
                link(nc.vector.tensor_tensor(score, af, rb, ALU.add))
                by_group = score.rearrange("p (g e) -> p e g", e=4)
                pairs = [(0, 1), (0, 2), (0, 3), (1, 2), (1, 3), (2, 3)]
                for n, (a, b) in enumerate(pairs):
                    if n == 0:
                        link(nc.vector.tensor_tensor(w8[:, 0:4], by_group[:, a, :], by_group[:, b, :], ALU.add))
                        continue
                    link(nc.vector.tensor_tensor(m8[:, 0:4], by_group[:, a, :], by_group[:, b, :], ALU.add))
                    link(nc.vector.tensor_tensor(w8[:, 0:4], w8[:, 0:4], m8[:, 0:4], ALU.max))
                link(nc.vector.max(m8, w8))
                link(nc.vector.max_index(idx[:, :], m8, w8))
                link(nc.vector.tensor_copy(gi, idx[:, 0:1]))
                link(nc.vector.tensor_scalar(emask, grp, gi, None, ALU.is_equal))
                link(nc.vector.tensor_tensor(score, score, emask, ALU.mult))
                link(nc.vector.tensor_scalar(emask, emask, -NEG, NEG, ALU.mult, ALU.add))
                link(nc.vector.tensor_tensor(score, score, emask, ALU.add))
                link(nc.vector.max(m8, score))
                link(nc.vector.max_index(idx[:, :], m8, score))
                link(nc.vector.tensor_copy(m8[:, 0:2], idx[:, 0:2]))
                link(nc.vector.tensor_scalar(emask, iota, m8[:, 0:1], None, ALU.is_equal))
                link(nc.vector.tensor_scalar(score, iota, m8[:, 1:2], None, ALU.is_equal))
                link(nc.vector.tensor_tensor(emask, emask, score, ALU.add))
                link(nc.vector.tensor_tensor_reduce(out=score, in0=emask, in1=af, scale=1.0, scalar=0.0, op0=ALU.mult,
                                                    op1=ALU.add, accum_out=gi))
                link(nc.vector.reciprocal(gi, gi))
                ins = nc.vector.tensor_scalar(cb, score, gi, None, ALU.mult)
                if tt == 0:
                    link(ins)
            ins.then_inc(W["combine"], 1)
            dve.wait_ge(L["comb"], 16)
            dve.wait_ge(W["y_ready"], 1)
            groups("moe", expert_up, NE, G1, Y, False, 4)
            dve.wait_ge(emptied["D"], OWN.count("D"))
            for c in range(DC):
                nc.vector.scalar_tensor_tensor(pool[:, H + c, :], pool[:, Y + c, :], mod[:, 80 + c:81 + c],
                                               pool[:, H + c, :], ALU.mult, ALU.add).then_inc(W["first_out"], 1)
            dve.wait_ge(W["first_out"], DC)
            root("final2", D)
            for c in range(DC):
                nc.vector.scalar_tensor_tensor(pool[:, H + c, :], pool[:, H + c, :], pc("final2_g", c), rstd[:, :],
                                               ALU.mult, ALU.mult).then_inc(W["final_ready"], 1)

        @block.gpsimd
        def _(pl):
            def toeplitz(dst, dram, base, rows, cols):
                pl.dma_start(dst, bass.AP(dram.tensor, base, [[dram.shape[2] - 1, rows], [1, cols]]))\
                    .then_inc(bias_landed[slot_[0]], 16)

            slot_ = [0]

            def load_bias(units, u, at, scratch):
                unit, slot = units[u], (at + u) % 2
                slot_[0] = slot
                if not bias_dmas(unit):
                    return
                wait(pl, W["max_ready"], at + u - 1)
                b0, b1 = pool[:, scratch + 8 + 2 * slot, :], pool[:, scratch + 9 + 2 * slot, :]
                if unit["kind"] == "local":
                    base = unit["head"] * 64 * 513 + 256
                    for r in range(2):
                        toeplitz(b0[64 * r:64 * r + 64, 0:64 + 64 * r], rel_rev, base - 64 * r, 64, 64 + 64 * r)
                        toeplitz(b1[64 * r:64 * r + 64, 0:192 + 64 * r], rel_rev, base - P - 64 * r, 64, 192 + 64 * r)
                else:
                    base = unit["row"] * P * 512 + 255
                    toeplitz(b0[:, 0:P], fbias_d, base, P, P)
                    toeplitz(b1[:, :], fbias_d, base - P, P, S)

            def attend(units, at, scratch):
                n = len(units)
                for u in range(2):
                    load_bias(units, u, at, scratch)
                for u in range(n):
                    unit, slot = units[u], (at + u) % 2
                    pl.wait_ge(W["recip_ready"], at + u + 1)
                    for qt in range(2):
                        w = {"mem": S, "cmp": NCMP}.get(unit["kind"], S if qt else P)
                        j = 2 * slot + qt
                        p = pool[:, scratch + j, 0:w]
                        last = nc.gpsimd.tensor_scalar(p, p, rden[:, j:j + 1], 1.0, ALU.mult, ALU.mult)
                    last.then_inc(W["probs_ready"], 1)
                    if u + 2 < n:
                        load_bias(units, u + 2, at, scratch)

            pl.dma_start(sinks, sinks_d.partition_broadcast(P)).then_inc(L["sinks"], 16)
            pl.dma_start(rb, rbias_d.partition_broadcast(P)).then_inc(L["sinks"], 16)
            pl.dma_start(grp, grp_d[:, 0:NE]).then_inc(L["sinks"], 16)
            pl.dma_start(iota, grp_d[:, NE:2 * NE]).then_inc(L["sinks"], 16)
            pl.dma_start(cm_add, cmpmask_d[:, 0:2 * NCMP]).then_inc(L["sinks"], 16)
            pl.dma_start(cm_mul, cmpmask_d[:, 2 * NCMP:4 * NCMP]).then_inc(L["sinks"], 16)
            pl.wait_ge(W["act_lo_ready"], split_end("x"))
            for slot in range(2):
                nc.gpsimd.memset(pool[0:64, SC1 + 8 + 2 * slot, 64:P], NEG)
                ins = nc.gpsimd.memset(pool[0:64, SC1 + 9 + 2 * slot, 192:S], NEG)
            ins.then_inc(W["masks_set"], 1)
            attend(MEM_UNITS, 0, SC1)
            attend(LOCAL_UNITS, 4, SC1)
            pl.wait_ge(W["merged_ready"], HC)
            pl.dma_start(chunks(H, DC), x_d).then_inc(L["x_again"], 16)
            pl.wait_ge(W["act_lo_ready"], split_end("merged"))
            pl.dma_start(flat(GDRAW, 2)[:, 0:384], gd_d).then_inc(L["gd"], 16)
            pl.wait_ge(W["act_lo_ready"], split_end("ffn"))
            for s in range(2):
                pl.dma_start(flat(ADA + 8 * s, 8), ada_tiles[s]).then_inc(ada_landed[s], 16)
            with pl.Fori(0, 4 * (G1 + 1) - 1) as i:
                for s in range(2):
                    pl.wait_ge(W["ada_used"], 2 * i + (s + 1))
                    pl.dma_start(flat(ADA + 8 * s, 8), ada_tiles[2 * i + (2 + s)]).then_inc(ada_landed[s], 16)
            pl.wait_ge(W["ada_used"], 8 * (G1 + 1))
            pl.dma_start(flat(Q2, 1)[0:32, 0:32], tab_d).then_inc(L["tables"], 16)
            pl.dma_start(flat(Q2 + 1, 2)[0:32, :], onehot_d).then_inc(L["tables"], 16)
            pl.dma_start(flat(Q2 + 3, 2)[0:32, :], maskrow_d).then_inc(L["tables"], 16)
            pl.wait_ge(W["hidden_lo"], G1)
            pl.dma_start(flat(28, 1)[:, 0:64], w2_d[0]).then_inc(L["cmp"], 16)
            pl.dma_start(flat(28, 1)[:, 64:P], w2_d[0]).then_inc(L["cmp"], 16)
            pl.dma_start(flat(28, 1)[:, P:P + 64], w2_d[1]).then_inc(L["cmp"], 16)
            for j in range(2):
                pl.dma_start(flat(29, 1)[64 * j:64 * j + 64, 0:64], pe_d).then_inc(L["cmp"], 16)
            pl.wait_ge(W["bias_rows_copied"], 1)
            pl.dma_start(fbias_d, flat(Q2 + 5, 2)[0:32, :].unsqueeze(1).to_broadcast([32, P, 512])).then_inc(W["bias_rows_stored"], 16)
            pl.wait_ge(W["bias_rows_stored"], 16)
            pl.wait_ge(W["act_lo_ready"], split_end("norm1"))
            for n in range(4):
                wait(pl, W["cmp_hidden"], n)
                for j in range(2):
                    pl.dma_start(flat(W1, 8)[64 * j:64 * j + 64, :], w1_d[n]).then_inc(L["w1"], 16)
            pl.wait_ge(W["cmp_hidden"], 4)
            attend(SECOND_UNITS, 20, SC2)
            pl.wait_ge(W["head_out"], 52)
            pl.dma_start(flat(RRAW, 1)[:, 0:256], router_d).then_inc(L["router"], 16)
            pl.wait_ge(W["act_lo_ready"], split_end("norm2"))
            nc.gpsimd.memset(chunks(Y, DC), 0.0).then_inc(W["y_ready"], 1)
            pl.wait_ge(W["combine_copied"], 1)
            pl.dma_start(comb_d, pool[0:NE, RRAW + 2, :]).then_inc(W["combine_stored"], 16)
            pl.wait_ge(W["combine_stored"], 16)
            pl.dma_start(chunks(COMB, NE), comb_d.partition_broadcast(P)).then_inc(L["comb"], 16)
            pl.wait_ge(L["comb"], 16)


SMALL_LOADS = 6
INPUTS = ["tiles", "ada_tiles", "x", "mem", "params", "rel_rev", "onehot", "maskrow", "ident", "cmpmask",
          "tab", "sinks", "rbias", "router", "gd", "w1", "w2", "pe", "grp"]


def bucket(dist):
    dist = np.maximum(dist, 0)
    large = 16 + (np.log(np.maximum(dist, 1).astype(np.float32) / np.float32(16))
                  / np.float32(np.log(2048 / 16)) * np.float32(16)).astype(np.int32)
    return np.where(dist < 16, dist, np.minimum(large, 31))


def constants():
    dist = 255 - np.arange(512)
    onehot = (bucket(dist)[None, :] == np.arange(32)[:, None]).astype(np.float32)
    causal = np.where(dist >= 0, 0.0, NEG)
    held = (dist >= 0) * ((dist <= 128).astype(int) + (dist % 4 == 0) + (dist % 16 == 0))
    dilated = np.where(held > 0, np.log(np.maximum(held, 1)), NEG)
    window = np.where((dist >= 0) & (dist <= 127), 0.0, NEG)
    maskrow = np.repeat(np.stack([dilated, window, causal, causal]), 8, axis=0).astype(np.float32)
    q = np.arange(P)[:, None, None] + P * np.arange(2)[None, :, None]
    seen = 16 * np.arange(NCMP)[None, None, :] + 31 <= q
    cmpmask = np.concatenate([np.where(seen, 0.0, NEG).reshape(P, -1), seen.reshape(P, -1)], axis=1)
    grp = np.tile(np.concatenate([np.arange(NE) // 4, np.arange(NE)]), (P, 1))
    return dict(onehot=onehot, maskrow=maskrow, ident=np.eye(P, dtype=np.float32),
                cmpmask=cmpmask.astype(np.float32), grp=grp.astype(np.float32))


def layout(a):
    def chunk_cols(v):
        return v.reshape(-1, P).T

    def fm(x):
        return np.ascontiguousarray(x.T.reshape(-1, P, x.shape[0]).transpose(1, 0, 2))

    def cut(w, kc, nc_):
        k, n = w.shape
        t = w.reshape(k // (kc * P), kc, P, n // (nc_ * P), nc_, P)
        return t.transpose(3, 0, 2, 4, 1, 5).reshape(-1, P, 2048)

    def down(w):
        k, n = w.shape
        t = w.reshape(k // 512, 4, P, n // 512, 4, P)
        return t.transpose(0, 3, 2, 4, 1, 5).reshape(-1, P, 2048)

    def pairs(a_, b_):
        return np.stack([a_, b_], axis=1).reshape(-1, P, 2048)

    def grouped(up, dn):
        n = len(dn) // 4
        up, dn = up.reshape(n, 8, P, 2048), dn.reshape(n, 4, P, 2048)
        parts = [up[0]]
        for g in range(1, n):
            parts += [up[g, 0:4], dn[g - 1], up[g, 4:8]]
        return parts + [dn[n - 1]]

    a = {k: np.asarray(v) for k, v in a.items()}
    w_in = a["w_in"][0]
    kv = cut(a["w_mem_kv"][0], 16, 1)
    t = cut(w_in, 16, 1)
    ca, cg, q, k, v, qm, gates = t[0:8], t[8:16], t[16:24], t[24:32], t[32:40], t[40:48], t[48:96]
    up = cut(a["w_up"][0], 16, 1)
    two = a["w_in_2"][0]
    o = np.cumsum([0, 512, 512, 512, 512, 128, 128, 512, 512, 512, 512, 128, 128, 128, 128, 128, 128, 24])
    part = [two[:, o[n]:o[n + 1]] for n in range(17)]

    def heads(w):
        return w.reshape(D, 8, 64)[:, KV_ORDER].reshape(D, 512)

    def rows(w):
        w = w.reshape(4, 8, 64, -1).copy()
        for m in (1, 3):
            w[m] = w[m][KV_ORDER]
        return w.reshape(D, -1)

    second = np.concatenate([part[0], heads(part[3]), part[6], heads(part[9]), part[1], part[7], part[4], part[10],
                             part[12], part[14], part[2], part[8], part[11], part[5], part[13], part[15]], axis=1)
    eg, eu, ed = a["exp_w_gate_2"][0], a["exp_w_up_2"][0], a["exp_w_down_2"][0]
    experts = np.concatenate([pairs(cut(eg[e], 16, 1), cut(eu[e], 16, 1)) for e in range(NE)])
    out = dict()
    out["tiles"] = np.concatenate(
        [kv, qm, q, k, v, pairs(cg, ca), gates, cut(a["w_attn_out"][0], 8, 2), cut(a["w_mem_out"][0], 8, 2),
         cut(a["w_conv_out"][0], 8, 2), cut(a["w_o"][0], 16, 1)]
        + grouped(pairs(up[0:FC], up[FC:]), down(a["w_down"][0]))
        + [cut(second, 16, 1), cut(rows(a["w_out_2"][0]), 16, 1)]
        + grouped(experts, down(ed.reshape(NE * 512, D))))
    assert out["tiles"].shape == (NT, P, 2048)
    ada = a["ada_w_2"][0].reshape(8, 2, P, 12, 1024)
    out["ada_tiles"] = ada.transpose(3, 0, 2, 1, 4).reshape(96, P, 2048)
    out["x"], out["mem"] = fm(a["x"][0]), fm(a["mem"][0])
    by_name = dict(
        mem_norm_g=a["mem_norm_g"], mix_norm_g=a["mix_norm_g"], ffn_norm_g=a["ffn_norm_g"],
        final_norm_g=a["final_norm_g"], norm1_g=a["norm1_g_2"], norm2_g=a["norm2_g_2"],
        mix2_g=rows(a["mix_norm_g_2"][0].reshape(D, 1)), final2_g=a["final_g_2"], gate_b=a["gate_b"],
        conv_b=a["conv_b"], ln_g=a["conv_ln_g"], ln_b=a["conv_ln_b"], ada_b=a["ada_b_2"], c=a["c_2"],
        fconv_w=a["ffn_conv_w"][0].reshape(3, 2, FC, P).transpose(0, 2, 1, 3),
        fconv_b=a["ffn_conv_b"][0].reshape(2, FC, P).transpose(1, 0, 2), conv_w=a["conv_w"])
    out["params"] = np.concatenate([chunk_cols(by_name[n].reshape(-1)) for n, _ in PARAMS], axis=1)
    out["rel_rev"] = np.tile(a["rel_bias"][0][:, None, ::-1], (1, 64, 1))
    out["tab"] = a["rel_bias_2"]
    out["sinks"] = a["sinks_2"][0]
    out["rbias"] = a["router_bias_2"]
    out["router"] = a["router_w_2"].reshape(DC, P, NE).transpose(1, 0, 2).reshape(P, -1)
    out["gd"] = part[16].reshape(DC, P, 24).transpose(1, 0, 2).reshape(P, -1)

    def w1(w):
        return w[0].reshape(2, 16, 64, P).transpose(0, 2, 1, 3).reshape(2, 64, 2048)

    out["w1"] = np.concatenate([w1(a["nsa_cmp_w1_k_2"]), w1(a["nsa_cmp_w1_v_2"])])
    out["w2"] = np.concatenate([a["nsa_cmp_w2_k_2"], a["nsa_cmp_w2_v_2"]])
    out["pe"] = np.concatenate([a["nsa_pe_k_2"][0].T, a["nsa_pe_v_2"][0].T], axis=1)
    out.update(constants())
    return out


def kernel(**inputs):
    import concourse.bacc as _bacc
    from concourse.bass_utils import run_bass_kernel_spmd as _run

    nc = _bacc.Bacc("TRN2", target_bir_lowering=False, num_devices=1)
    laid = layout(inputs)
    arrays, args = {}, []
    for name in INPUTS:
        arrays[name + "_dram"] = np.ascontiguousarray(laid[name])
        args.append(nc.dram_tensor(name + "_dram", laid[name].shape, F32, kind="ExternalInput").ap())
    out = nc.dram_tensor("out_dram", (P, DC, S), F32, kind="ExternalOutput").ap()
    fbias = nc.dram_tensor("bias_rows_dram", (32, P, 512), F32, kind="Internal").ap()
    comb = nc.dram_tensor("combine_dram", (NE, S), F32, kind="Internal").ap()
    build(nc, *args, out, fbias, comb)
    r = _run(nc, [arrays], core_ids=[0])
    y = r.results[0]["out_dram"]
    return y.transpose(2, 1, 0).reshape(1, S, D)
```

```python
from contextlib import ExitStack, contextmanager

import numpy as np

import concourse.bass as bass
from concourse import mybir

F32 = mybir.dt.float32
F32R = mybir.dt.float32r
U32 = mybir.dt.uint32
ALU = mybir.AluOpType
ACT = mybir.ActivationFunctionType
AX = mybir.AxisListType

P = 128
S = 256
D = 2048
DC = D // P
HALF = D // 2
HC = HALF // P
TAPS = 31
PAD = TAPS - 1
DFF = 5632
FC = DFF // P
G1 = FC // 4
NE = 16
EPS = 1e-6
NEG = -1e30
NCMP = (S - 32) // 16 + 1
RAW = 2
SPL = 4
AHEAD = SPL - 1
POOLC = 75

PHASES = [("km", HC, "A"), ("vm", HC, "A"), ("qm", HC, "A"), ("q", HC, "A"), ("k", HC, "A"),
          ("v", HC, "A"), ("glu", 2 * HC, "A"), ("gates", 3 * DC, "A"), ("ya", HC, "D"),
          ("ym", HC, "D"), ("yc", HC, "D"), ("wo", DC, "D"), ("ffn", 12 * G1, None),
          ("q2", 16, "A"), ("k2", 12, "A"), ("mixed2", 4, "A"), ("v2", 8, "A"), ("wout", DC, "D"),
          ("moe", 12 * NE, None)]


def owners():
    own = ""
    for _, n, who in PHASES:
        if who:
            own += who * n
        else:
            own += "A" * 8 + "AAAADDDDAAAA" * (n // 12 - 1) + "DDDD"
    return own


OWN = owners()
NT = len(OWN)
BASE = {}
_at = 0
for _name, _n, _ in PHASES:
    BASE[_name] = _at
    _at += _n

PARAMS = [("mem_norm_g", 16), ("mix_norm_g", 16), ("ffn_norm_g", 16), ("final_norm_g", 16),
          ("norm1_g", 16), ("norm2_g", 16), ("mix2_g", 16), ("final2_g", 16), ("gate_b", 48),
          ("conv_b", 8), ("ln_g", 8), ("ln_b", 8), ("ada_b", 96), ("c", 16),
          ("fconv_w", 3 * 88), ("fconv_b", 88), ("conv_w", TAPS * 8)]
PCOL = {}
_at = 0
for _name, _n in PARAMS:
    PCOL[_name] = (_at, _n)
    _at += _n
NPAR = _at


class Tile:

    def __init__(self, k, i=None, n=0, body=None):
        self.k, self.i, self.n, self.body = k, i, n, k if body is None else body

    def __add__(self, m):
        return Tile(self.k + m, self.i, self.n, self.body)

    def plus(self, value, slope):
        return value if self.i is None else value + slope * self.i

    def count(self):
        return self.plus(self.k + 1, self.n)

    def emptied(self, who):
        if self.i is None:
            return OWN[:max(self.k + 1, 0)].count(who)
        each = OWN[self.body:self.body + self.n].count(who)
        if each == 0:
            return OWN[:self.k + 1 + self.n].count(who)
        return OWN[:self.k + 1 + self.n].count(who) - each + each * self.i


class Tally:

    def __init__(self, sem):
        self.sem, self.n, self.i, self.per = sem, 0, None, 0

    def value(self):
        return self.n if self.i is None else self.n + self.per * self.i

    def add(self, ins):
        ins.then_inc(self.sem, 1)
        self.n += 1
        return self.value()

    @contextmanager
    def loop(self, i, per, rounds):
        self.i, self.per, began = i, per, self.n
        yield
        assert self.n - began == per, (self.n - began, per)
        self.i, self.n = None, began + per * rounds


def wait(eng, sem, value):
    if not isinstance(value, int) or value > 0:
        eng.wait_ge(sem, value)


KV_ORDER = [0, 4, 1, 5, 2, 6, 3, 7]
MEM_UNITS = [dict(kind="mem", q=2 * h, k=2 * h, v=2 * h) for h in range(4)]
LOCAL_UNITS = [dict(kind="local", q=h // 2, half=h % 2, k=h // 2, v=h // 2, head=h) for h in range(16)]


def second_units():
    out = []
    for h in range(8):
        out.append(dict(kind="causal", q=h // 2, half=h % 2, k=h // 2, v=h // 2, row=h))
    for h in range(8):
        g = KV_ORDER[h]
        out.append(dict(kind="sink", q=4 + h // 2, half=h % 2, k=8, v=9, row=8 + g, head=g))
    for h in range(8):
        out.append(dict(kind="causal", q=8 + h // 2, half=h % 2, k=4 + h // 2, v=4 + h // 2, row=16 + h))
    for h in range(8):
        g = KV_ORDER[h]
        base = dict(q=12 + h // 2, half=h % 2, row=24 + g)
        out.append(dict(kind="causal", k=10, v=10, gate=3 * g + 1, part=0, **base))
        out.append(dict(kind="causal", k=11, v=11, gate=3 * g + 2, part=1, **base))
        out.append(dict(kind="cmp", k=None, v=None, gate=3 * g, part=2, **base))
    return out


SECOND_UNITS = second_units()
ALL_UNITS = MEM_UNITS + LOCAL_UNITS + SECOND_UNITS


def bias_dmas(unit):
    return {"mem": 0, "cmp": 0, "local": 4}.get(unit["kind"], 2)


def bias_total(u):
    return sum(bias_dmas(x) for x in ALL_UNITS[u % 2:u + 1:2])


NORMS = [("mem", 16), ("x", 16), ("lnmean", 8), ("lnvar", 8), ("ffn", 16), ("final", 16),
         ("norm1", 16), ("mixa", 4), ("mixb", 4), ("mixc", 4), ("mixd", 4), ("norm2", 16), ("final2", 16)]
NORM_AT = {n: k for k, (n, _) in enumerate(NORMS)}
PRE_AT, _at = {}, 0
for _name, _n in NORMS:
    PRE_AT[_name] = _at
    _at += 0 if _name == "lnmean" else _n
SQ_AT, _at = {}, 0
for _name, _n in NORMS:
    SQ_AT[_name] = _at
    _at += 0 if _name == "lnmean" else _n // 4
SPLITS = [("mem", 16), ("x", 16), ("oa", 8), ("om", 8), ("cv", 8), ("merged", 16), ("ffn", 16),
          ("norm1", 16), ("mixa", 4), ("mixb", 4), ("mixc", 4), ("mixd", 4), ("norm2", 16)]
SPLIT_AT, _at = {}, 0
for _name, _n in SPLITS:
    SPLIT_AT[_name] = (_at, _n)
    _at += _n


def split_end(name):
    return sum(SPLIT_AT[name])


ADA_STEPS = {step: j for j, step in enumerate([1, 2, 4, 5, 6, 8, 9, 10])}


def build(nc, tiles, ada_tiles, x_d, mem_d, params_d, rel_rev, onehot_d, maskrow_d, ident_d,
          cmpmask_d, tab_d, sinks_d, rbias_d, router_d, gd_d, w1_d, w2_d, pe_d, grp_d, out, fbias_d, comb_d):
    with ExitStack() as ctx:
        def sb(name, shape, dt=F32):
            return ctx.enter_context(nc.sbuf_tensor(name, shape, dt))

        def ps(name, shape):
            return ctx.enter_context(nc.psum_tensor(name, shape, F32))

        def sem(name):
            return ctx.enter_context(nc.semaphore(name))

        raw = sb("raw", [P, RAW, 2048])
        w_hi = sb("w_hi", [P, SPL, 2048], F32R)
        w_lo = sb("w_lo", [P, SPL, 2048], F32R)
        a_hi = sb("a_hi", [P, DC, S], F32R)
        a_lo = sb("a_lo", [P, DC, S], F32R)
        h_hi = sb("h_hi", [P, 4, S], F32R)
        h_lo = sb("h_lo", [P, 4, S], F32R)
        pool = sb("pool", [P, POOLC, S])
        par = sb("par", [P, NPAR])
        ones = sb("ones", [P, P])
        ident = sb("ident", [P, P])
        small = sb("small", [P, 724])
        rstd = sb("rstd", [P, S])
        var = sb("var", [P, S])
        mod = sb("mod", [P, 96])
        scale1 = sb("scale1", [P, DC])
        scale2 = sb("scale2", [P, DC])
        cact = sb("cact", [P, DC])
        idx = sb("idx", [P, 8], U32)

        psT = ps("psT", [P, 2, 1024])
        psS = ps("psS", [P, 2, 512])
        psP = ps("psP", [P, 512])
        psO = ps("psO", [P, 512])
        psN = psO[:, 0:S]

        landed = [sem(f"tile_landed{s}") for s in range(RAW)]
        hi_done, lo_done, used = sem("tile_hi_done"), sem("tile_lo_done"), sem("tile_multiplied")
        emptied = {"A": sem("sums_emptied_act"), "D": sem("sums_emptied_dve")}
        L = {n: sem(f"loaded_{n}") for n in
             ("par", "mem", "x", "x_again", "ident", "tables", "sinks", "w1", "cmp", "gd", "router", "comb")}
        names = ["ones_set", "squares_ready", "sums_part", "variance_ready", "std_ready", "normed_ready",
                 "act_hi_ready", "act_lo_ready", "scores_ready", "max_ready", "exp_ready", "recip_ready",
                 "probs_ready", "probs_transposed", "probs_copied", "pv_ready", "head_out", "centered",
                 "conv_in", "conv_done", "dve_step", "merged_ready", "taps_done",
                 "silu_done", "pairs_read", "hidden_hi", "hidden_lo", "ada_used", "ada_added", "ada_scaled", 
                 "ada_sums", "ada_copied", "bias_rows", "bias_rows_copied",
                 "bias_rows_stored", "gd_hi", "gd_lo", "gd_sums", "gd_ready", "cmp_in", "cmp_hidden",
                 "cmp_gelu", "cmp_tanh", "cmp_out", "cmp_ready", "cv_silu", "router_hi",
                 "router_lo", "router_sums", "affinity", "combine", "combine_tr", "combine_copied",
                 "combine_stored", "y_ready", "output_stored", "final_ready", "masks_set", "c_act",
                 "first_out", "mean_sums", "cmp_sums"]
        W = {n: sem(n) for n in names}
        bias_landed = [sem(f"bias_landed{i}") for i in range(2)]
        ada_landed = [sem(f"ada_landed{i}") for i in range(4)]

        def pc(name, j=None, n=1):
            at, width = PCOL[name]
            if j is None:
                return par[:, at:at + width]
            return par[:, at + j:at + j + n] if isinstance(j, int) else par[:, bass.ds(j + at, n)]

        def chunks(a, n):
            return pool[:, a:a + n, :]

        def flat(a, n):
            return pool[:, a:a + n, :].rearrange("p c s -> p (c s)")

        X, MEMX, KM, VM = 0, 16, 32, 40
        QM, Q, CV = 48, 56, 64
        K, V = 16, 24
        SQ = 64
        SQLN = 48
        GLU = 44
        B0, B1, B2 = 0, 16, 32
        H = 32
        ADA, ADACC = (0, 8, 52, 62), 16
        ADA_LAST, ADACC_LAST = 64, 56
        US, YS, HF = 20, 25, 48
        PRE = 0
        Q2, K2, V2, W1, KP = 0, 16, 48, 64, 30
        SC1, SC2 = (0, 8, 12), (60, 28, 68)
        ROWS = 72
        Y, COMB, ES = 0, 16, 52
        GDRAW, RRAW = 60, 60
        slots = flat(CV, 11)[:, 0:(HC + 1) * (S + PAD)].rearrange("p (c s) -> p c s", c=HC + 1)
        hp = slots[:, 1:HC + 1, :]

        cv = slots[:, 0:HC, 0:S]

        def one(name, src, c):
            return cv[:, c, :] if name in ("cv", "lnvar") else pool[:, src + c, :]
        us = flat(US, 5)[:, 0:4 * (S + 2)].rearrange("p (c s) -> p c s", c=4)

        _cols = [0]

        def col(n):
            _cols[0] += n
            return small[:, _cols[0] - n:_cols[0]]

        mx, nmx, den, rden = col(8), col(8), col(8), col(8)
        sinks, esink = col(8), col(8)
        gd = col(48)
        cm_add, cm_mul = col(2 * NCMP), col(2 * NCMP)
        zero = col(1)
        kc_sb = col(NCMP)
        vc_sb = col(P)[0:NCMP, :]
        rb, grp = col(NE), col(NE)
        aff = col(2 * NE)
        w8, m8, gi = col(8), col(8), col(1)
        score, emask, comb = col(NE), col(NE), col(2 * NE)
        iota = col(NE)
        c_x, c_u, c_g = col(2 * NCMP), col(2 * NCMP), col(2 * NCMP)

        block = ctx.enter_context(nc.Block())

        @block.sync
        def _(sp):
            def load_tile(t):
                wait(sp, lo_done, (t + -RAW).count())
                sp.dma_start(raw[:, t.k % RAW, :], tiles[t.k if t.i is None else t.i * t.n + t.k])\
                    .then_inc(landed[t.k % RAW], 16)

            def toeplitz(dst, dram, base, rows, cols, slot):
                sp.dma_start(dst, bass.AP(dram.tensor, base, [[dram.shape[2] - 1, rows], [1, cols]]))\
                    .then_inc(bias_landed[slot], 16)

            def load_bias(units, u, at, scratch):
                unit, slot = units[u], (at + u) % 2
                if not bias_dmas(unit):
                    return
                wait(sp, W["max_ready"], at + u - 1)
                b0, b1 = pool[:, scratch[2] + 2 * slot, :], pool[:, scratch[2] + 1 + 2 * slot, :]
                if unit["kind"] == "local":
                    base = unit["head"] * 64 * 513 + 256
                    for r in range(2):
                        toeplitz(b0[64 * r:64 * r + 64, 0:64 + 64 * r], rel_rev, base - 64 * r, 64, 64 + 64 * r, slot)
                        toeplitz(b1[64 * r:64 * r + 64, 0:192 + 64 * r], rel_rev, base - P - 64 * r, 64, 192 + 64 * r, slot)
                else:
                    base = unit["row"] * P * 512 + 255
                    toeplitz(b0[:, 0:P], fbias_d, base, P, P, slot)
                    toeplitz(b1[:, :], fbias_d, base - P, P, S, slot)

            def load_tiles(first, end):
                with sp.Fori(0, (end - first) // 4) as i:
                    for k in range(4):
                        load_tile(Tile(first + k, i, 4))

            for k in range(4):
                load_tile(Tile(k))
            load_tiles(4, BASE["glu"] + 4)
            sp.wait_ge(W["masks_set"], 1)
            for u in range(len(LOCAL_UNITS)):
                load_bias(LOCAL_UNITS, u, 4, SC1)
            load_tiles(BASE["glu"] + 4, BASE["wout"] + 4)
            sp.wait_ge(W["bias_rows_stored"], 16)
            sp.wait_ge(W["cmp_hidden"], 4)
            for u in range(len(SECOND_UNITS)):
                load_bias(SECOND_UNITS, u, 20, SC2)
            load_tiles(BASE["wout"] + 4, NT)
            for g in range(4):
                sp.wait_ge(W["final_ready"], 4 * g + 4)
                sp.dma_start(out[:, 4 * g:4 * g + 4, :], chunks(H + 4 * g, 4)).then_inc(W["output_stored"], 16)
            sp.wait_ge(W["output_stored"], 64)

        @block.scalar
        def _(act):
            def split(t):
                if t.i is None and t.k >= NT:
                    return
                wait(act, used, (t + -SPL).count())
                act.wait_ge(landed[t.k % RAW], t.plus(16 * (t.k // RAW + 1), 16 * (t.n // RAW)))
                nc.scalar.activation(w_hi[:, t.k % SPL, :], raw[:, t.k % RAW, :], ACT.Copy).then_inc(hi_done, 1)

            def sums(t, n=S):
                act.wait_ge(used, t.count())
                return psT[:, t.k % 2, 0:n]

            def linear(name, n, dest, scale):
                peeled = 4 if name == "km" else 0
                for k in range(peeled):
                    split(Tile(k + AHEAD))
                    nc.scalar.activation(pool[:, dest + k, :], sums(Tile(k)), ACT.Copy, scale=scale)\
                        .then_inc(emptied["A"], 1)
                with act.Fori(0, (n - peeled) // 4) as i:
                    for k in range(4):
                        t = Tile(BASE[name] + peeled + k, i, 4)
                        split(t + AHEAD)
                        nc.scalar.activation(pool[:, bass.ds(i * 4 + (dest + peeled + k), 1), :], sums(t), ACT.Copy,
                                             scale=scale).then_inc(emptied["A"], 1)

            def token_sums(t, s, dest):
                act.wait_ge(used, (t + 3).count())
                for tt in range(2):
                    ins = nc.scalar.activation(pool[:, dest:dest + 4, tt * P:tt * P + P],
                                               psT[:, s, tt * 512:tt * 512 + 512].rearrange("p (c s) -> p c s", c=4),
                                               ACT.Copy)
                ins.then_inc(emptied["A"], 4)

            def token_major(name, dest):
                for s in range(2):
                    t = Tile(BASE[name] + 4 * s)
                    for k in range(4):
                        split(t + k + AHEAD)
                    token_sums(t, s, dest + 4 * s)

            def others(name, n):
                with act.Fori(0, n // 4) as i:
                    for k in range(4):
                        split(Tile(BASE[name] + k, i, 4) + AHEAD)

            def squares(name, src, sq=SQ, after=None):
                n = dict(NORMS)[name]
                for g in range(n // 4):
                    at = SQ_AT[name] + g
                    wait(act, W["sums_part"], at - 1)
                    if after:
                        act.wait_ge(W[after[0]], after[1] + 4 * g + 4)
                    nc.scalar.activation(chunks(sq + 4 * (at % 2), 4), (cv[:, 4 * g:4 * g + 4, :] if name == "lnvar" else chunks(src + 4 * g, 4)),
                                         ACT.Square).then_inc(W["squares_ready"], 1)

            def std(name):
                act.wait_ge(W["variance_ready"], NORM_AT[name] + 1)
                nc.scalar.activation(var[:, :], var[:, :], ACT.Sqrt).then_inc(W["std_ready"], 1)

            def norm(name, src, sq=SQ, after=None, first_tiles=False):
                squares(name, src, sq, after)
                if first_tiles:
                    for k in range(AHEAD):
                        split(Tile(k))
                std(name)

            def hi(name, src, dst, bias=None, pre=None):
                for c in range(SPLIT_AT[name][1]):
                    if pre:
                        act.wait_ge(W["normed_ready"], PRE_AT[pre] + c + 1)
                    nc.scalar.activation(a_hi[:, dst + c, :], one(name, src, c), ACT.Identity,
                                         bias=zero if bias is None else bias[:, c:c + 1])\
                        .then_inc(W["act_hi_ready"], 1)

            def attend(units, at, scratch):
                n = len(units)
                for u in range(n + 3):
                    if u < n:
                        unit, slot = units[u], (at + u) % 2
                        act.wait_ge(W["max_ready"], at + u + 1)
                        for qt in range(2):
                            w = {"mem": S, "cmp": NCMP}.get(unit["kind"], S if qt else P)
                            j = 2 * ((at + u) % 4) + qt
                            dst = pool[:, scratch[0] + j, 0:w]
                            src = psS[:, slot, qt * S:qt * S + w] if unit["kind"] == "mem" else dst
                            kw = {} if unit["kind"] == "cmp" else dict(accum_out=den[:, j:j + 1])
                            last = nc.scalar.activation(dst, src, ACT.Exp, bias=nmx[:, j:j + 1], **kw)
                            if unit["kind"] == "sink":
                                h = unit["head"]
                                last = nc.scalar.activation(esink[:, j:j + 1], nmx[:, j:j + 1], ACT.Exp,
                                                            bias=sinks[:, h:h + 1])
                        last.then_inc(W["exp_ready"], 1)
                    if u >= 3:
                        v = u - 3
                        unit, slot = units[v], (at + v) % 2
                        act.wait_ge(W["probs_transposed"], at + v + 1)
                        wait(act, W["pv_ready"], at + v - 1)
                        dst = flat(scratch[1] + 2 * slot, 2)
                        if unit["kind"] == "cmp":
                            ins = nc.scalar.activation(dst[0:NCMP, 0:S], psP[0:NCMP, 0:S], ACT.Copy)
                        else:
                            w = 2 * S if unit["kind"] == "mem" else S + P
                            ins = nc.scalar.activation(dst[:, 0:w], psP[:, 0:w], ACT.Copy)
                        ins.then_inc(W["probs_copied"], 1)

            act.dma_start(chunks(MEMX, DC), mem_d).then_inc(L["mem"], 16)
            act.dma_start(par[:, :], params_d).then_inc(L["par"], 16)
            act.dma_start(chunks(X, DC), x_d).then_inc(L["x"], 16)
            act.dma_start(ident[:, :], ident_d).then_inc(L["ident"], 16)

            act.wait_ge(L["mem"], 16)
            act.wait_ge(W["ones_set"], 3)
            norm("mem", MEMX, first_tiles=True)
            hi("mem", MEMX, 0, pre="mem")
            linear("km", HC, KM, 1.0)
            token_major("vm", VM)
            act.wait_ge(L["x"], 16)
            norm("x", X)
            act.wait_ge(used, BASE["qm"])
            hi("x", X, 0, pre="x")
            linear("qm", HC, QM, 1.0 / 16)
            attend(MEM_UNITS, 0, SC1)
            linear("q", HC, Q, 1.0 / 8)
            linear("k", HC, K, 1.0)
            token_major("v", V)
            attend(LOCAL_UNITS, 4, SC1)
            with act.Fori(0, HC // 2) as i:
                for k in range(4):
                    t = Tile(BASE["glu"] + k, i, 4)
                    split(t + AHEAD)
                    if k % 2 == 0:
                        act.wait_ge(W["conv_in"], 2 * i + (k // 2 + 1))
                    nc.scalar.activation(pool[:, GLU + k, :], sums(t), ACT.Copy if k % 2 else ACT.Sigmoid)\
                        .then_inc(emptied["A"], 1)
            act.wait_ge(W["head_out"], 20)
            act.wait_ge(W["conv_in"], 2 + HC)
            with act.Fori(0, 4) as i:
                for k in range(12):
                    t = Tile(BASE["gates"] + k, i, 12)
                    split(t + AHEAD)
                    nc.scalar.activation(pool[:, bass.ds(12 * i + k, 1), :], sums(t), ACT.Sigmoid,
                                         bias=pc("gate_b", 12 * i + k)).then_inc(emptied["A"], 1)
            hi("oa", Q, 8)
            hi("om", QM, 0)
            act.wait_ge(W["centered"], 1)
            act.wait_ge(W["act_lo_ready"], split_end("om"))
            norm("lnvar", CV, SQLN)
            others("ya", HC)
            for c in range(HC):
                act.wait_ge(W["normed_ready"], PRE_AT["lnvar"] + c + 1)
                nc.scalar.activation(cv[:, c, :], cv[:, c, :], ACT.Silu,
                                     bias=pc("ln_b", c)).then_inc(W["cv_silu"], 1)
            act.wait_ge(W["cv_silu"], HC)
            act.wait_ge(used, BASE["ym"])
            hi("cv", CV, 8)
            others("ym", HC)
            others("yc", HC)
            act.wait_ge(W["merged_ready"], 2 * HC)
            hi("merged", B1, 0)
            others("wo", DC)
            act.wait_ge(emptied["D"], OWN[:BASE["ffn"]].count("D"))
            norm("ffn", H)
            act.wait_ge(used, BASE["ffn"])
            hi("ffn", PRE, 0, pre="ffn")

            def ada_scale(j, g):
                act.wait_ge(ada_landed[j % 4], 32 * g + 16 * (j // 4 + 1))
                for r in range(2):
                    part = flat(ADA[j % 4] + 4 * r, 4)
                    ins = nc.scalar.activation(part, part, ACT.Copy, scale=cact[:, 2 * j + r:2 * j + r + 1])
                ins.then_inc(W["ada_scaled"], 1)

            def ffn_up(t, g, half, row):
                for k in range(4):
                    split(t + k + AHEAD)
                    f = 8 * g + (4 * half + k)
                    if k % 2 == 0:
                        act.wait_ge(W["pairs_read"], 4 * g + (2 * half + k // 2 + 1))
                    src = sums(t + k)
                    nc.scalar.activation(us[:, k, 2:2 + S], src, ACT.Copy)
                    nc.scalar.activation(pool[:, YS + k, :], src, ACT.Identity, scale=row("fconv_w", 2 * 88 + f),
                                         bias=row("fconv_b", f)).then_inc(emptied["A"], 1)
                    if k % 2:
                        act.wait_ge(W["taps_done"], 8 * g + (4 * half + k + 1))
                        nc.scalar.activation(pool[:, YS + k, :], pool[:, YS + k, :], ACT.Silu)\
                            .then_inc(W["silu_done"], 1)
                    if isinstance(g, int):
                        ada_scale(4 * half + k, 0)
                    elif 8 * half + k in ADA_STEPS:
                        ada_scale(ADA_STEPS[8 * half + k], g)

            def expert_up(t, g, half, row):
                for k in range(4):
                    split(t + k + AHEAD)
                    if k % 2 == 0:
                        act.wait_ge(W["pairs_read"], 4 * g + (4 * G1 + 2 * half + k // 2 + 1))
                    nc.scalar.activation(pool[:, ES + k, :], sums(t + k), ACT.Copy if k % 2 else ACT.Silu)\
                        .then_inc(emptied["A"], 1)

            def hidden_hi(t, g, before):
                act.wait_ge(W["pairs_read"], 4 * g + (4 * before + 6))
                act.wait_ge(used, t.count())
                nc.scalar.activation(h_hi[:, :, :], chunks(HF, 4), ACT.Copy).then_inc(W["hidden_hi"], 1)

            def groups(name, up, n, before, ada):
                b = BASE[name]
                for half in range(2):
                    up(Tile(b + 4 * half), 0, half, pc)
                hidden_hi(Tile(b + 7), 0, before)
                with act.Fori(0, n - 1) as i:
                    t = Tile(b + 8, i, 12)
                    up(t, i + 1, 0, pc)
                    for k in range(4):
                        split(t + 4 + k + AHEAD)
                        if ada and 4 + k in ADA_STEPS:
                            ada_scale(ADA_STEPS[4 + k], i + 1)
                    up(t + 8, i + 1, 1, pc)
                    hidden_hi(t + 11, i + 1, before)
                for k in range(4):
                    split(Tile(b + 12 * n - 4 + k) + AHEAD)

            act.wait_ge(L["par"], 16)
            nc.scalar.activation(cact[:, :], pc("c"), ACT.Silu).then_inc(W["c_act"], 1)
            act.wait_ge(W["c_act"], 1)
            groups("ffn", ffn_up, G1, 0, True)
            act.wait_ge(emptied["D"], OWN[:BASE["q2"]].count("D"))
            norm("final", H, US)
            norm("norm1", H, US, after=("normed_ready", PRE_AT["final"]))
            act.wait_ge(used, BASE["q2"])
            hi("norm1", PRE, 0, bias=mod[:, 0:16], pre="norm1")
            linear("q2", 16, Q2, 1.0 / 8)
            linear("k2", 12, K2, 1.0)
            act.wait_ge(L["gd"], 16)
            hflat = h_hi[:, :, :].rearrange("p c s -> p (c s)")
            nc.scalar.activation(hflat[:, 0:384], flat(GDRAW, 2)[:, 0:384], ACT.Copy).then_inc(W["gd_hi"], 1)
            for k in range(12):
                t = Tile(BASE["mixed2"] + k)
                split(t + AHEAD)
                if k in (5, 10):
                    act.wait_ge(W["cmp_gelu"], 1 if k == 5 else 3)
                    nc.scalar.activation(c_u, c_u, ACT.Tanh, scale=float(np.sqrt(2 / np.pi)))\
                        .then_inc(W["cmp_tanh"], 1)
                if k == 8:
                    act.wait_ge(W["gd_sums"], 1)
                    nc.scalar.activation(gd, psO[:, 0:48], ACT.Sigmoid).then_inc(W["gd_ready"], 1)
                if k < 4:
                    nc.scalar.activation(pool[:, V2 + 8 + k, :], sums(t), ACT.Copy).then_inc(emptied["A"], 1)
                elif k % 4 == 3:
                    token_sums(t + -3, k // 8, V2 + 4 * (k // 8))
            attend(SECOND_UNITS, 20, SC2)
            act.wait_ge(W["head_out"], 52)
            squares("mixa", Q2)
            for m in range(4):
                name = "mix" + "abcd"[m]
                std(name)
                if m < 3:
                    squares("mix" + "bcd"[m], Q2 + 4 * (m + 1))
                hi(name, Q2 + 4 * m, 4 * m, pre=name)
            others("wout", DC)
            act.wait_ge(emptied["D"], OWN[:BASE["moe"]].count("D"))
            norm("norm2", H)
            act.wait_ge(used, BASE["moe"])
            hi("norm2", PRE, 0, bias=mod[:, 48:64], pre="norm2")
            act.wait_ge(L["router"], 16)
            nc.scalar.activation(hflat[:, 0:256], flat(RRAW, 1)[:, 0:256], ACT.Copy).then_inc(W["router_hi"], 1)
            act.wait_ge(W["router_sums"], 1)
            nc.scalar.activation(aff, psO[:, 0:32], ACT.Sigmoid).then_inc(W["affinity"], 1)
            act.wait_ge(W["combine_tr"], 1)
            nc.scalar.activation(pool[0:NE, RRAW + 2, :], psP[0:NE, 0:S], ACT.Copy).then_inc(W["combine_copied"], 1)
            groups("moe", expert_up, NE, G1, False)
            norm("final2", H, after=("first_out", 0))

        @block.tensor
        def _(pe):
            def begin(t):
                pe.wait_ge(lo_done, t.count())
                for who in "AD":
                    wait(pe, emptied[who], (t + -2).emptied(who))

            def three(ps_out, w, x_hi, x_lo, k, first, last):
                slot = w.k % SPL
                wh, wl = w_hi[:, slot, k * P:k * P + P], w_lo[:, slot, k * P:k * P + P]
                nc.tensor.matmul(ps_out, wh, x_hi, start=first, stop=False)
                nc.tensor.matmul(ps_out, wh, x_lo, start=False, stop=False)
                return nc.tensor.matmul(ps_out, wl, x_hi, start=False, stop=last)

            def chunk_split(name, k):
                if name:
                    pe.wait_ge(W["act_lo_ready"], SPLIT_AT[name][0] + k + 1)

            def feature_major(t, fresh=None):
                begin(t)
                for k in range(DC):
                    chunk_split(fresh, k)
                    last = three(psT[:, t.k % 2, 0:S], t, a_hi[:, k, :], a_lo[:, k, :], k, k == 0, k == DC - 1)
                last.then_inc(used, 1)

            def token_major(t):
                begin(t)
                slot = t.k % SPL
                for tt in range(2):
                    dst = psT[:, t.k % 2, tt * P:tt * P + P]
                    for k in range(DC):
                        xh, xl = a_hi[:, k, tt * P:tt * P + P], a_lo[:, k, tt * P:tt * P + P]
                        wh, wl = w_hi[:, slot, k * P:k * P + P], w_lo[:, slot, k * P:k * P + P]
                        nc.tensor.matmul(dst, xh, wh, start=k == 0, stop=False)
                        nc.tensor.matmul(dst, xh, wl, start=False, stop=False)
                        last = nc.tensor.matmul(dst, xl, wh, start=False, stop=k == DC - 1)
                last.then_inc(used, 1)

            def quad_part(t, j, s):
                pe.wait_ge(lo_done, (t + j).count())
                if j == 0:
                    for who in "AD":
                        wait(pe, emptied[who], (t + (-5 if s else -2)).emptied(who))
                slot = (t + j).k % SPL
                for i in range(4):
                    k = 4 * j + i
                    for tt in range(2):
                        dst = psT[:, s, tt * 512:tt * 512 + 512]
                        xh, xl = a_hi[:, k, tt * P:tt * P + P], a_lo[:, k, tt * P:tt * P + P]
                        wh, wl = w_hi[:, slot, 512 * i:512 * i + 512], w_lo[:, slot, 512 * i:512 * i + 512]
                        nc.tensor.matmul(dst, xh, wh, start=k == 0, stop=False)
                        nc.tensor.matmul(dst, xh, wl, start=False, stop=False)
                        last = nc.tensor.matmul(dst, xl, wh, start=False, stop=k == DC - 1)
                last.then_inc(used, 1)

            def quads(name):
                for s in range(2):
                    for j in range(4):
                        quad_part(Tile(BASE[name] + 4 * s), j, s)

            def half_width(t, a, fresh=None):
                begin(t)
                for n in range(2):
                    for k in range(HC):
                        chunk_split(fresh if n == 0 else None, k)
                        last = three(psT[:, t.k % 2, n * S:n * S + S], t, a_hi[:, a + k, :], a_lo[:, a + k, :],
                                     HC * n + k, k == 0, k == HC - 1)
                last.then_inc(used, 1)

            def down(t):
                begin(t)
                for n in range(4):
                    for k in range(4):
                        last = three(psT[:, t.k % 2, n * S:n * S + S], t, h_hi[:, k, :], h_lo[:, k, :],
                                     4 * n + k, k == 0, k == 3)
                last.then_inc(used, 1)

            def tiles_of(name, n, multiply, *args, fresh=None):
                peeled = 4 if fresh else 0
                for k in range(peeled):
                    multiply(Tile(BASE[name] + k), *args, fresh=None if k else fresh)
                with pe.Fori(0, (n - peeled) // 4) as i:
                    for k in range(4):
                        multiply(Tile(BASE[name] + peeled + k, i, 4), *args)

            def norm(name, sq=SQ):
                n = dict(NORMS)[name]
                wait(pe, W["variance_ready"], NORM_AT[name])
                for g in range(n // 4):
                    at = SQ_AT[name] + g
                    pe.wait_ge(W["squares_ready"], at + 1)
                    for c in range(4):
                        last = nc.tensor.matmul(psN, ones[:, :], pool[:, sq + 4 * (at % 2) + c, :],
                                                start=g == 0 and c == 0, stop=g == n // 4 - 1 and c == 3)
                    last.then_inc(W["sums_part"], 1)

            def outs_before(units, u):
                return sum(x.get("part") in (None, 2) for x in units[:u])

            def attend(units, at, scratch, q0, k0, v0, outs):
                n = len(units)
                for u in range(n + 4):
                    if u < n:
                        unit, slot = units[u], (at + u) % 2
                        mem = u >= 2 and units[u - 2]["kind"] == "mem"
                        wait(pe, W["exp_ready"] if mem else W["max_ready"], at + u - 1)
                        for qt in range(2):
                            dst = psS[:, slot, qt * S:qt * S + S]
                            if unit["kind"] == "mem":
                                for c in range(2):
                                    last = nc.tensor.matmul(dst, pool[:, q0 + unit["q"] + c, qt * P:qt * P + P],
                                                            pool[:, k0 + unit["k"] + c, :], start=c == 0, stop=c == 1)
                                continue
                            r = 64 * unit["half"]
                            q = pool[r:r + 64, q0 + unit["q"], qt * P:qt * P + P]
                            if unit["kind"] == "cmp":
                                last = nc.tensor.matmul(dst[:, 0:NCMP], q, kc_sb[r:r + 64, :], start=True, stop=True)
                            else:
                                w = S if qt else P
                                last = nc.tensor.matmul(dst[:, 0:w], q, pool[r:r + 64, k0 + unit["k"], 0:w],
                                                        start=True, stop=True)
                        last.then_inc(W["scores_ready"], 1)
                    if 3 <= u < n + 3:
                        v = u - 3
                        unit, slot = units[v], (at + v) % 2
                        pe.wait_ge(W["probs_ready"], at + v + 1)
                        wait(pe, W["probs_copied"], at + v)
                        for qt in range(2):
                            p = pool[:, scratch[0] + 2 * ((at + v) % 4) + qt, :]
                            if unit["kind"] == "cmp":
                                last = nc.tensor.transpose(psP[0:NCMP, qt * P:qt * P + P], p[:, 0:NCMP], ident[:, :])
                                continue
                            last = nc.tensor.transpose(psP[:, qt * P:qt * P + P], p[:, 0:P], ident[:, :])
                            if unit["kind"] == "mem":
                                last = nc.tensor.transpose(psP[:, S + qt * P:S + qt * P + P], p[:, P:S], ident[:, :])
                            elif qt:
                                last = nc.tensor.transpose(psP[:, S:S + P], p[:, P:S], ident[:, :])
                        last.then_inc(W["probs_transposed"], 1)
                    if u >= 4:
                        v = u - 4
                        unit, slot = units[v], (at + v) % 2
                        pe.wait_ge(W["probs_copied"], at + v + 1)
                        part = unit.get("part")
                        if part in (None, 0):
                            wait(pe, W["head_out"], outs + outs_before(units, v))
                        pT = flat(scratch[1] + 2 * slot, 2)
                        if unit["kind"] == "mem":
                            for c in range(2):
                                for kt in range(2):
                                    last = nc.tensor.matmul(psO[:, c * S:c * S + S],
                                                            pool[:, v0 + unit["v"] + c, kt * P:kt * P + P],
                                                            pT[:, kt * S:kt * S + S], start=kt == 0, stop=kt == 1)
                        elif unit["kind"] == "cmp":
                            last = nc.tensor.matmul(psO[:, 0:S], vc_sb, pT[0:NCMP, 0:S], start=False, stop=True)
                        else:
                            vv = pool[:, v0 + unit["v"], :]
                            nc.tensor.matmul(psO[:, 0:S], vv[:, 0:P], pT[:, 0:S], start=part in (None, 0), stop=False)
                            last = nc.tensor.matmul(psO[:, P:S], vv[:, P:S], pT[:, S:S + P], start=False,
                                                    stop=part is None)
                        last.then_inc(W["pv_ready"], 1)

            pe.wait_ge(W["ones_set"], 3)
            norm("mem")
            tiles_of("km", HC, feature_major, fresh="mem")
            quads("vm")
            norm("x")
            tiles_of("qm", HC, feature_major, fresh="x")
            pe.wait_ge(L["ident"], 16)
            pe.wait_ge(emptied["A"], BASE["q"])
            pe.wait_ge(W["variance_ready"], 2)
            attend(MEM_UNITS, 0, SC1, QM, KM, VM, 0)
            tiles_of("q", HC, feature_major)
            tiles_of("k", HC, feature_major)
            quads("v")
            pe.wait_ge(emptied["A"], BASE["glu"])
            attend(LOCAL_UNITS, 4, SC1, Q, K, V, 4)
            tiles_of("glu", 2 * HC, feature_major)
            tiles_of("gates", 3 * DC, feature_major)
            pe.wait_ge(W["conv_done"], HC)
            pe.wait_ge(W["head_out"], 20)
            for c in range(HC):
                last = nc.tensor.matmul(psN, ones[:, :], cv[:, c, :], start=c == 0, stop=c == HC - 1)
            last.then_inc(W["mean_sums"], 1)
            norm("lnvar", SQLN)
            tiles_of("ya", HC, half_width, 8, fresh="oa")
            tiles_of("ym", HC, half_width, 0, fresh="om")
            tiles_of("yc", HC, half_width, 8, fresh="cv")
            tiles_of("wo", DC, feature_major, fresh="merged")
            norm("ffn")

            def ada_reduce(g, acc=ADACC):
                pe.wait_ge(W["ada_used"], 8 * g + 8)
                for m in range(8):
                    last = nc.tensor.matmul(psP[:, m:m + 1], flat(acc, 4)[:, m * P:m * P + P], ones[:, 0:1],
                                            start=True, stop=True)
                last.then_inc(W["ada_sums"], 1)

            def groups(name, n, before, ada):
                b = BASE[name]
                for k in range(8):
                    feature_major(Tile(b + k), "ffn" if ada and k == 0 else None)
                with pe.Fori(0, n - 1) as i:
                    t = Tile(b + 8, i, 12)
                    for k in range(4):
                        feature_major(t + k)
                        if ada and k == 1:
                            ada_reduce(i)
                    pe.wait_ge(W["hidden_lo"], i + (before + 1))
                    for k in range(4):
                        down(t + 4 + k)
                    for k in range(4):
                        feature_major(t + 8 + k)
                if ada:
                    ada_reduce(n - 1)
                pe.wait_ge(W["hidden_lo"], before + n)
                for k in range(4):
                    down(Tile(b + 12 * n - 4 + k))

            groups("ffn", G1, 0, True)
            norm("final", US)
            pe.wait_ge(L["tables"], 48)
            pe.wait_ge(W["ada_copied"], G1)
            nc.tensor.matmul(psP[0:32, :], flat(Q2, 1)[0:32, 0:32], flat(Q2 + 1, 2)[0:32, :], start=True, stop=True)\
                .then_inc(W["bias_rows"], 1)
            norm("norm1", US)
            tiles_of("q2", 16, feature_major, fresh="norm1")
            tiles_of("k2", 12, feature_major)
            hh = h_hi[:, :, :].rearrange("p c s -> p (c s)")
            hl = h_lo[:, :, :].rearrange("p c s -> p (c s)")

            def narrow(n):
                for tt in range(2):
                    for k in range(DC):
                        xh, xl = a_hi[:, k, tt * P:tt * P + P], a_lo[:, k, tt * P:tt * P + P]
                        dst = psO[:, tt * n:tt * n + n]
                        nc.tensor.matmul(dst, xh, hh[:, k * n:k * n + n], start=k == 0, stop=False)
                        nc.tensor.matmul(dst, xh, hl[:, k * n:k * n + n], start=False, stop=False)
                        last = nc.tensor.matmul(dst, xl, hh[:, k * n:k * n + n], start=False, stop=k == DC - 1)
                return last

            def cmp_hidden(r, part):
                if part == 0:
                    pe.wait_ge(W["cmp_in"], r + 1)
                    wait(pe, W["cmp_sums"], r)
                pe.wait_ge(L["w1"], 32 * (2 * r + part + 1))
                for j in range(2):
                    for i in range(16):
                        last = nc.tensor.matmul(psS[:, j, 0:NCMP], flat(W1, 8)[64 * j:64 * j + 64, i * P:i * P + P],
                                                flat(KP, 2)[64 * j:64 * j + 64,
                                                            (16 * part + i) * NCMP:(16 * part + i + 1) * NCMP],
                                                start=part == 0 and i == 0, stop=part == 1 and i == 15)
                last.then_inc(W["cmp_hidden"], 1)

            def cmp_out(r):
                pe.wait_ge(W["cmp_gelu"], 2 * r + 2)
                if r == 0:
                    nc.tensor.matmul(psP[:, 0:2 * NCMP], flat(28, 1)[:, 0:P], c_g, start=True, stop=True)\
                        .then_inc(W["cmp_out"], 1)
                    return
                pe.wait_ge(W["cmp_ready"], 1)
                for j in range(2):
                    last = nc.tensor.matmul(psP[0:NCMP, 64 * j:64 * j + 64], c_g[:, NCMP * j:NCMP * j + NCMP],
                                            flat(28, 1)[:, P:P + 64], start=True, stop=True)
                last.then_inc(W["cmp_out"], 1)

            for k in range(12):
                if k in (1, 3, 5, 8):
                    cmp_hidden(k // 5, 0 if k in (1, 5) else 1)
                if k in (6, 11):
                    cmp_out(k // 11)
                if k == 7:
                    pe.wait_ge(W["gd_lo"], 1)
                    pe.wait_ge(W["variance_ready"], NORM_AT["norm1"] + 1)
                    narrow(24).then_inc(W["gd_sums"], 1)
                t = Tile(BASE["mixed2"] + k)
                if k == 0:
                    feature_major(t)
                elif k < 4:
                    token_major(t)
                else:
                    quad_part(t + -(k % 4), k % 4, k // 8)
            pe.wait_ge(W["gd_ready"], 1)
            pe.wait_ge(W["cmp_ready"], 2)
            pe.wait_ge(emptied["A"], OWN[:BASE["wout"]].count("A"))
            attend(SECOND_UNITS, 20, SC2, Q2, K2, V2, 20)
            for m in range(4):
                if m == 0:
                    pe.wait_ge(W["head_out"], 52)
                norm("mix" + "abcd"[m])
            tiles_of("wout", DC, feature_major, fresh="mixa")
            norm("norm2")
            pe.wait_ge(W["act_lo_ready"], split_end("norm2"))
            pe.wait_ge(W["router_lo"], 1)
            pe.wait_ge(W["variance_ready"], NORM_AT["norm2"] + 1)
            narrow(NE).then_inc(W["router_sums"], 1)
            pe.wait_ge(W["combine"], 1)
            for tt in range(2):
                last = nc.tensor.transpose(psP[0:NE, tt * P:tt * P + P], comb[:, tt * NE:tt * NE + NE], ident[:, :])
            last.then_inc(W["combine_tr"], 1)
            groups("moe", NE, G1, False)
            ada_reduce(G1, ADACC_LAST)
            pe.wait_ge(W["affinity"], 1)
            norm("final2")

        @block.vector
        def _(dve):
            step = Tally(W["dve_step"])

            def link(ins):
                dve.wait_ge(step.sem, step.add(ins))

            def lo(t):
                if t.i is None and t.k >= NT:
                    return
                dve.wait_ge(hi_done, t.count())
                nc.vector.tensor_tensor(w_lo[:, t.k % SPL, :], raw[:, t.k % RAW, :],
                                        w_hi[:, t.k % SPL, :].bitcast(F32), ALU.subtract).then_inc(lo_done, 1)

            def others(name, n):
                with dve.Fori(0, n // 4) as i:
                    for k in range(4):
                        lo(Tile(BASE[name] + k, i, 4) + AHEAD)

            def root(name, width):
                m = NORM_AT[name]
                dve.wait_ge(W["sums_part"], SQ_AT[name] + dict(NORMS)[name] // 4)
                nc.vector.tensor_scalar(var[:, :], psN, 1.0 / width, EPS, ALU.mult, ALU.add)\
                    .then_inc(W["variance_ready"], 1)
                dve.wait_ge(W["std_ready"], m + (1 if m < NORM_AT["lnmean"] else 0))
                link(nc.vector.reciprocal(rstd[:, :], var[:, :]))

            def normed(name, src, dst, gain):
                for c in range(dict(NORMS)[name]):
                    nc.vector.scalar_tensor_tensor(one(name, dst, c), one(name, src, c), gain[:, c:c + 1],
                                                   rstd[:, :], ALU.mult, ALU.mult).then_inc(W["normed_ready"], 1)

            def act_lo(name, src, dst, bias=None):
                for c in range(SPLIT_AT[name][1]):
                    dve.wait_ge(W["act_hi_ready"], SPLIT_AT[name][0] + c + 1)
                    nc.vector.scalar_tensor_tensor(a_lo[:, dst + c, :], one(name, src, c),
                                                   zero if bias is None else bias[:, c:c + 1],
                                                   a_hi[:, dst + c, :].bitcast(F32), ALU.add, ALU.subtract)\
                        .then_inc(W["act_lo_ready"], 1)

            def attend(units, at, scratch, q0):
                n = len(units)
                for u in range(n + 5):
                    if u >= 5:
                        v = u - 5
                        unit = units[v]
                        if unit.get("part") in (None, 2):
                            dve.wait_ge(W["pv_ready"], at + v + 1)
                            if unit["kind"] == "mem":
                                ins = nc.vector.tensor_copy(chunks(q0 + unit["q"], 2).rearrange("p c s -> p (c s)"),
                                                            psO[:, :])
                            else:
                                r = 64 * unit["half"]
                                ins = nc.vector.tensor_copy(pool[r:r + 64, q0 + unit["q"], :], psO[r:r + 64, 0:S])
                            ins.then_inc(W["head_out"], 1)
                    if u < n:
                        unit, slot = units[u], (at + u) % 2
                        dve.wait_ge(W["scores_ready"], at + u + 1)
                        wait(dve, W["probs_transposed"], at + u - 3)
                        if bias_dmas(unit):
                            dve.wait_ge(bias_landed[slot], 16 * bias_total(at + u))
                        for qt in range(2):
                            w = {"mem": S, "cmp": NCMP}.get(unit["kind"], S if qt else P)
                            j = 2 * ((at + u) % 4) + qt
                            src = psS[:, slot, qt * S:qt * S + w]
                            if unit["kind"] == "mem":
                                link(nc.vector.reduce_max(mx[:, j:j + 1], src, AX.X))
                            else:
                                add = cm_add[:, qt * NCMP:qt * NCMP + NCMP] if unit["kind"] == "cmp" else \
                                    pool[:, scratch[2] + 2 * slot + qt, 0:w]
                                link(nc.vector.tensor_tensor_reduce(
                                    out=pool[:, scratch[0] + j, 0:w], in0=src, in1=add, scale=1.0, scalar=-3.0e38,
                                    op0=ALU.add, op1=ALU.max, accum_out=mx[:, j:j + 1]))
                        if unit["kind"] == "sink":
                            h = unit["head"]
                            for qt in range(2):
                                j = 2 * ((at + u) % 4) + qt
                                ins = nc.vector.tensor_tensor(mx[:, j:j + 1], mx[:, j:j + 1], sinks[:, h:h + 1], ALU.max)
                            link(ins)
                        j = 2 * ((at + u) % 4)
                        nc.vector.tensor_scalar(nmx[:, j:j + 2], mx[:, j:j + 2], -1.0, None, ALU.mult).then_inc(W["max_ready"], 1)
                    if 1 <= u < n + 1:
                        v = u - 1
                        unit, slot = units[v], (at + v) % 2
                        j = 2 * ((at + v) % 4)
                        dve.wait_ge(W["exp_ready"], at + v + 1)
                        if unit["kind"] == "cmp":
                            for qt in range(2):
                                e = pool[:, scratch[0] + j + qt, 0:NCMP]
                                link(nc.vector.tensor_tensor_reduce(
                                    out=e, in0=e, in1=cm_mul[:, qt * NCMP:qt * NCMP + NCMP], scale=1.0, scalar=0.0,
                                    op0=ALU.mult, op1=ALU.add, accum_out=den[:, j + qt:j + qt + 1]))
                            link(nc.vector.tensor_scalar(den[:, j:j + 2], den[:, j:j + 2],
                                                         float(np.finfo(np.float32).tiny), None, ALU.max))
                        if unit["kind"] == "sink":
                            link(nc.vector.tensor_tensor(den[:, j:j + 2], den[:, j:j + 2], esink[:, j:j + 2], ALU.add))
                        ins = nc.vector.reciprocal(rden[:, j:j + 2], den[:, j:j + 2])
                        if "gate" in unit:
                            link(ins)
                            for qt in range(2):
                                g = 24 * qt + unit["gate"]
                                ins = nc.vector.tensor_tensor(rden[:, j + qt:j + qt + 1], rden[:, j + qt:j + qt + 1],
                                                              gd[:, g:g + 1], ALU.mult)
                        ins.then_inc(W["recip_ready"], 1)

            nc.vector.memset(ones[:, :], 1.0).then_inc(W["ones_set"], 1)
            nc.vector.memset(zero, 0.0).then_inc(W["ones_set"], 1)
            nc.vector.memset(w8, -3.0e38).then_inc(W["ones_set"], 1)
            dve.wait_ge(W["ones_set"], 3)

            dve.wait_ge(L["par"], 16)
            for k in range(AHEAD):
                lo(Tile(k))
            root("mem", D)
            normed("mem", MEMX, MEMX, pc("mem_norm_g"))
            act_lo("mem", MEMX, 0)
            others("km", HC)
            others("vm", HC)
            root("x", D)
            normed("x", X, X, pc("mix_norm_g"))
            act_lo("x", X, 0)
            others("qm", HC)
            attend(MEM_UNITS, 0, SC1, QM)
            others("q", HC)
            others("k", HC)
            others("v", HC)
            attend(LOCAL_UNITS, 4, SC1, Q)
            nc.vector.memset(hp[:, :, 0:PAD], 0.0).then_inc(W["conv_in"], 2)
            with dve.Fori(0, HC // 2) as i:
                for k in range(4):
                    t = Tile(BASE["glu"] + k, i, 4)
                    lo(t + AHEAD)
                    if k % 2:
                        dve.wait_ge(emptied["A"], t.emptied("A"))
                        nc.vector.tensor_tensor(hp[:, bass.ds(2 * i + k // 2, 1), PAD:PAD + S], pool[:, GLU + k - 1, :],
                                                pool[:, GLU + k, :], ALU.mult).then_inc(W["conv_in"], 1)
            dve.wait_ge(W["conv_in"], 2 + HC)
            taps = [(j, tap) for j in range(2) for tap in range(TAPS)]
            with dve.Fori(0, 4) as i:
                with step.loop(i, 2 * TAPS - 2, 4):
                    for k in range(12):
                        lo(Tile(BASE["gates"] + k, i, 12) + AHEAD)
                        for j, tap in taps[len(taps) * k // 12:len(taps) * (k + 1) // 12]:
                            c = 2 * i + j
                            dst = cv[:, bass.ds(c, 1), :]
                            src = hp[:, bass.ds(c, 1), tap:tap + S]
                            w = pc("conv_w", 8 * tap + c)
                            if tap == 0:
                                if j:
                                    dve.wait_ge(W["conv_done"], c)
                                link(nc.vector.tensor_scalar(dst, src, w, pc("conv_b", c), ALU.mult, ALU.add))
                                continue
                            ins = nc.vector.scalar_tensor_tensor(dst, src, w, dst, ALU.mult, ALU.add)
                            if tap == TAPS - 1:
                                ins.then_inc(W["conv_done"], 1)
                                if j:
                                    dve.wait_ge(W["conv_done"], c + 1)
                            else:
                                link(ins)
            act_lo("oa", Q, 8)
            act_lo("om", QM, 0)
            dve.wait_ge(W["mean_sums"], 1)
            nc.vector.tensor_scalar(rstd[:, :], psN, 1.0 / HALF, None, ALU.mult).then_inc(W["variance_ready"], 1)
            dve.wait_ge(W["variance_ready"], NORM_AT["lnmean"] + 1)
            for c in range(HC):
                ins = nc.vector.tensor_tensor(cv[:, c, :], cv[:, c, :], rstd[:, :], ALU.subtract)
            ins.then_inc(W["centered"], 1)
            dve.wait_ge(W["centered"], 1)
            root("lnvar", HALF)
            normed("lnvar", CV, CV, pc("ln_g"))

            def gated(name, gates, into):
                with dve.Fori(0, HC // 4) as i:
                    for k in range(4):
                        t = Tile(BASE[name] + k, i, 4)
                        lo(t + AHEAD)
                        dve.wait_ge(used, t.count())
                        g = pool[:, bass.ds(8 * i + (gates + 2 * k), 2), :].rearrange("p c s -> p (c s)")
                        nc.vector.tensor_tensor(g, psT[:, t.k % 2, 0:2 * S], g, ALU.mult).then_inc(emptied["D"], 1)
                        if into is not None:
                            m = pool[:, bass.ds(8 * i + (into + 2 * k), 2), :].rearrange("p c s -> p (c s)")
                            dve.wait_ge(emptied["D"], t.emptied("D"))
                            nc.vector.tensor_tensor(m, m, g, ALU.add).then_inc(W["merged_ready"], 1)

            gated("ya", B1, None)
            dve.wait_ge(emptied["D"], HC)
            act_lo("cv", CV, 8)
            gated("ym", B2, B1)
            dve.wait_ge(W["merged_ready"], HC)
            gated("yc", B0, B1)
            dve.wait_ge(W["merged_ready"], 2 * HC)
            act_lo("merged", B1, 0)
            dve.wait_ge(L["x_again"], 16)
            with dve.Fori(0, DC // 4) as i:
                for k in range(4):
                    t = Tile(BASE["wo"] + k, i, 4)
                    lo(t + AHEAD)
                    dve.wait_ge(used, t.count())
                    h = pool[:, bass.ds(4 * i + (H + k), 1), :]
                    nc.vector.tensor_tensor(h, psT[:, t.k % 2, 0:S], h, ALU.add).then_inc(emptied["D"], 1)
            dve.wait_ge(emptied["D"], OWN[:BASE["ffn"]].count("D"))
            root("ffn", D)
            normed("ffn", H, PRE, pc("ffn_norm_g"))
            act_lo("ffn", PRE, 0)
            nc.vector.memset(us[:, :, 0:2], 0.0).then_inc(W["pairs_read"], 2)

            def ada_copy(g):
                dve.wait_ge(W["ada_sums"], g + 1)
                dst = mod[:, 8 * g:8 * g + 8] if isinstance(g, int) else mod[:, bass.ds(8 * g, 8)]
                nc.vector.tensor_copy(dst, psP[:, 0:8]).then_inc(W["ada_copied"], 1)

            def add_bias(g, end):
                dve.wait_ge(W["ada_copied"], end)
                m = mod[:, 8 * g:8 * end]
                link(nc.vector.tensor_tensor(m, m, pc("ada_b")[:, 8 * g:8 * end], ALU.add))

            def ffn_up(t, k, g, half):
                f = 8 * g + (4 * half + k)
                dve.wait_ge(emptied["A"], (t + k).emptied("A"))
                y = pool[:, YS + k, :]
                link(nc.vector.scalar_tensor_tensor(y, us[:, k, 1:1 + S], pc("fconv_w", 88 + f), y, ALU.mult, ALU.add))
                nc.vector.scalar_tensor_tensor(y, us[:, k, 0:S], pc("fconv_w", f), y, ALU.mult, ALU.add)\
                    .then_inc(W["taps_done"], 1)
                if k % 2:
                    dve.wait_ge(W["silu_done"], 4 * g + (2 * half + k // 2 + 1))
                    nc.vector.tensor_tensor(pool[:, HF + 2 * half + k // 2, :], y, pool[:, YS + k - 1, :], ALU.mult)\
                        .then_inc(W["pairs_read"], 1)

            def expert_up(t, k, g, half):
                if k % 2:
                    dve.wait_ge(emptied["A"], (t + k).emptied("A"))
                    h = pool[:, HF + 2 * half + k // 2, :]
                    w = pool[:, COMB + g, :] if isinstance(g, int) else pool[:, bass.ds(g + COMB, 1), :]
                    link(nc.vector.tensor_tensor(h, pool[:, ES + k - 1, :], pool[:, ES + k, :], ALU.mult))
                    nc.vector.tensor_tensor(h, h, w, ALU.mult).then_inc(W["pairs_read"], 1)

            def add_down(t, k, acc):
                dve.wait_ge(used, (t + k).count())
                a = flat(acc + 4 * k, 4)
                nc.vector.tensor_tensor(a, psT[:, (t + k).k % 2, :], a, ALU.add).then_inc(emptied["D"], 1)

            def hidden_lo(g):
                dve.wait_ge(W["hidden_hi"], g + 1)
                nc.vector.tensor_tensor(h_lo[:, :, :], chunks(HF, 4), h_hi[:, :, :].bitcast(F32), ALU.subtract)\
                    .then_inc(W["hidden_lo"], 1)
                dve.wait_ge(W["hidden_lo"], g + 1)

            def groups(name, up, n, before, acc, ada, links):
                b = BASE[name]
                for k in range(8):
                    lo(Tile(b + k) + AHEAD)
                    up(Tile(b + 4 * (k // 4)), k % 4, 0, k // 4)
                hidden_lo(before)
                with dve.Fori(0, n - 1) as i:
                    with step.loop(i, links, n - 1):
                        t = Tile(b + 8, i, 12)
                        for k in range(12):
                            lo(t + k + AHEAD)
                            if 4 <= k < 8:
                                add_down(t + 4, k - 4, acc)
                            else:
                                up(t + 4 * (k // 4), k % 4, i + 1, k // 8)
                            if ada and k == 2:
                                ada_copy(i)
                        hidden_lo(i + (before + 1))
                if ada:
                    ada_copy(n - 1)
                for k in range(4):
                    lo(Tile(b + 12 * n - 4 + k) + AHEAD)
                    add_down(Tile(b + 12 * n - 4), k, acc)

            groups("ffn", ffn_up, G1, 0, H, True, 8)
            dve.wait_ge(emptied["D"], OWN[:BASE["q2"]].count("D"))
            root("final", D)
            normed("final", H, H, pc("final_norm_g"))
            add_bias(0, G1)
            nc.vector.scalar_tensor_tensor(scale1[:, :], mod[:, 16:32], 1.0, pc("norm1_g"), ALU.add, ALU.mult)
            link(nc.vector.scalar_tensor_tensor(scale2[:, :], mod[:, 64:80], 1.0, pc("norm2_g"), ALU.add, ALU.mult))
            dve.wait_ge(W["bias_rows"], 1)
            nc.vector.tensor_tensor(flat(ROWS, 2)[0:32, :], psP[0:32, :], flat(Q2 + 3, 2)[0:32, :], ALU.add)\
                .then_inc(W["bias_rows_copied"], 1)
            root("norm1", D)
            normed("norm1", H, PRE, scale1)
            act_lo("norm1", PRE, 0, bias=mod[:, 0:16])
            others("q2", 16)
            others("k2", 12)
            dve.wait_ge(W["gd_hi"], 1)
            hl = h_lo[:, :, :].rearrange("p c s -> p (c s)")
            hh = h_hi[:, :, :].rearrange("p c s -> p (c s)").bitcast(F32)
            nc.vector.tensor_tensor(hl[:, 0:384], flat(GDRAW, 2)[:, 0:384], hh[:, 0:384], ALU.subtract)\
                .then_inc(W["gd_lo"], 1)

            def cmp_in(r):
                wait(dve, W["cmp_hidden"], 2 * r)
                src = pool[:, V2 + 8 if r else K2 + 9, :].rearrange("p (m b) -> p b m", b=16)
                pe_r = flat(29, 1)[:, 32 * r:32 * r + 32]
                for a in range(2):
                    ins = nc.vector.tensor_tensor(
                        flat(KP, 2)[:, 16 * a * NCMP:16 * (a + 1) * NCMP].rearrange("p (b m) -> p b m", b=16),
                        src[:, :, a:a + NCMP], pe_r[:, 16 * a:16 * a + 16].unsqueeze(2).to_broadcast([P, 16, NCMP]),
                        ALU.add)
                ins.then_inc(W["cmp_in"], 1)

            def gelu_in(r):
                dve.wait_ge(W["cmp_hidden"], 2 * r + 2)
                for j in range(2):
                    ins = nc.vector.tensor_copy(c_x[:, NCMP * j:NCMP * j + NCMP], psS[:, j, 0:NCMP])
                ins.then_inc(W["cmp_sums"], 1)
                dve.wait_ge(W["cmp_sums"], r + 1)
                link(nc.vector.tensor_tensor(c_u, c_x, c_x, ALU.mult))
                link(nc.vector.tensor_scalar(c_u, c_u, 0.044715, 1.0, ALU.mult, ALU.add))
                nc.vector.tensor_tensor(c_u, c_u, c_x, ALU.mult).then_inc(W["cmp_gelu"], 1)

            def gelu_out(r):
                dve.wait_ge(W["cmp_tanh"], r + 1)
                link(nc.vector.scalar_tensor_tensor(c_g, c_u, 1.0, c_x, ALU.add, ALU.mult))
                nc.vector.tensor_scalar(c_g, c_g, 0.5, None, ALU.mult).then_inc(W["cmp_gelu"], 1)

            def cmp_ready(r):
                dve.wait_ge(W["cmp_out"], r + 1)
                if r == 0:
                    for j in range(2):
                        ins = nc.vector.tensor_copy(kc_sb[64 * j:64 * j + 64, :],
                                                    psP[64 * j:64 * j + 64, NCMP * j:NCMP * j + NCMP])
                else:
                    ins = nc.vector.tensor_copy(vc_sb, psP[0:NCMP, 0:P])
                ins.then_inc(W["cmp_ready"], 1)

            dve.wait_ge(L["cmp"], 80)
            dve.wait_ge(emptied["A"], OWN[:BASE["k2"] + 10].count("A"))
            cmp_in(0)
            for k in range(12):
                lo(Tile(BASE["mixed2"] + k) + AHEAD)
                if k == 3:
                    gelu_in(0)
                    dve.wait_ge(emptied["A"], OWN[:BASE["mixed2"] + 1].count("A"))
                    cmp_in(1)
                elif k in (5, 10):
                    gelu_out(k // 10)
                elif k in (6, 11):
                    cmp_ready(k // 11)
                elif k == 8:
                    gelu_in(1)
            dve.wait_ge(L["sinks"], 16 * SMALL_LOADS)
            dve.wait_ge(W["gd_ready"], 1)
            attend(SECOND_UNITS, 20, SC2, Q2)
            dve.wait_ge(W["head_out"], 52)
            for m in range(4):
                name = "mix" + "abcd"[m]
                root(name, HALF // 2)
                normed(name, Q2 + 4 * m, Q2 + 4 * m, pc("mix2_g", 4 * m, 4))
                act_lo(name, Q2 + 4 * m, 4 * m)
            with dve.Fori(0, DC // 4) as i:
                for k in range(4):
                    t = Tile(BASE["wout"] + k, i, 4)
                    lo(t + AHEAD)
                    dve.wait_ge(used, t.count())
                    h = pool[:, bass.ds(4 * i + (H + k), 1), :]
                    nc.vector.scalar_tensor_tensor(h, psT[:, t.k % 2, 0:S], mod[:, bass.ds(4 * i + (32 + k), 1)], h,
                                                   ALU.mult, ALU.add).then_inc(emptied["D"], 1)
            dve.wait_ge(emptied["D"], OWN[:BASE["moe"]].count("D"))
            root("norm2", D)
            normed("norm2", H, PRE, scale2)
            act_lo("norm2", PRE, 0, bias=mod[:, 48:64])
            dve.wait_ge(W["router_hi"], 1)
            nc.vector.tensor_tensor(hl[:, 0:256], flat(RRAW, 1)[:, 0:256], hh[:, 0:256], ALU.subtract)\
                .then_inc(W["router_lo"], 1)
            dve.wait_ge(W["affinity"], 1)
            for tt in range(2):
                af, cb = aff[:, NE * tt:NE * tt + NE], comb[:, NE * tt:NE * tt + NE]
                link(nc.vector.tensor_tensor(score, af, rb, ALU.add))
                by_group = score.rearrange("p (g e) -> p e g", e=4)
                pairs = [(0, 1), (0, 2), (0, 3), (1, 2), (1, 3), (2, 3)]
                for n, (a, b) in enumerate(pairs):
                    if n == 0:
                        link(nc.vector.tensor_tensor(w8[:, 0:4], by_group[:, a, :], by_group[:, b, :], ALU.add))
                        continue
                    link(nc.vector.tensor_tensor(m8[:, 0:4], by_group[:, a, :], by_group[:, b, :], ALU.add))
                    link(nc.vector.tensor_tensor(w8[:, 0:4], w8[:, 0:4], m8[:, 0:4], ALU.max))
                link(nc.vector.max(m8, w8))
                link(nc.vector.max_index(idx[:, :], m8, w8))
                link(nc.vector.tensor_copy(gi, idx[:, 0:1]))
                link(nc.vector.tensor_scalar(emask, grp, gi, None, ALU.is_equal))
                link(nc.vector.tensor_tensor(score, score, emask, ALU.mult))
                link(nc.vector.tensor_scalar(emask, emask, -NEG, NEG, ALU.mult, ALU.add))
                link(nc.vector.tensor_tensor(score, score, emask, ALU.add))
                link(nc.vector.max(m8, score))
                link(nc.vector.max_index(idx[:, :], m8, score))
                link(nc.vector.tensor_copy(m8[:, 0:2], idx[:, 0:2]))
                link(nc.vector.tensor_scalar(emask, iota, m8[:, 0:1], None, ALU.is_equal))
                link(nc.vector.tensor_scalar(score, iota, m8[:, 1:2], None, ALU.is_equal))
                link(nc.vector.tensor_tensor(emask, emask, score, ALU.add))
                link(nc.vector.tensor_tensor_reduce(out=score, in0=emask, in1=af, scale=1.0, scalar=0.0, op0=ALU.mult,
                                                    op1=ALU.add, accum_out=gi))
                link(nc.vector.reciprocal(gi, gi))
                ins = nc.vector.tensor_scalar(cb, score, gi, None, ALU.mult)
                if tt == 0:
                    link(ins)
            ins.then_inc(W["combine"], 1)
            dve.wait_ge(L["comb"], 16)
            dve.wait_ge(W["y_ready"], 1)
            groups("moe", expert_up, NE, G1, Y, False, 4)
            ada_copy(G1)
            add_bias(G1, G1 + 1)
            dve.wait_ge(emptied["D"], OWN.count("D"))
            for c in range(DC):
                nc.vector.scalar_tensor_tensor(pool[:, H + c, :], pool[:, Y + c, :], mod[:, 80 + c:81 + c],
                                               pool[:, H + c, :], ALU.mult, ALU.add).then_inc(W["first_out"], 1)
            dve.wait_ge(W["first_out"], DC)
            root("final2", D)
            for c in range(DC):
                nc.vector.scalar_tensor_tensor(pool[:, H + c, :], pool[:, H + c, :], pc("final2_g", c), rstd[:, :],
                                               ALU.mult, ALU.mult).then_inc(W["final_ready"], 1)

        @block.gpsimd
        def _(pl):
            def attend(units, at, scratch):
                for u, unit in enumerate(units):
                    pl.wait_ge(W["recip_ready"], at + u + 1)
                    for qt in range(2):
                        w = {"mem": S, "cmp": NCMP}.get(unit["kind"], S if qt else P)
                        j = 2 * ((at + u) % 4) + qt
                        p = pool[:, scratch[0] + j, 0:w]
                        last = nc.gpsimd.tensor_scalar(p, p, rden[:, j:j + 1], 1.0, ALU.mult, ALU.mult)
                    last.then_inc(W["probs_ready"], 1)

            pl.dma_start(sinks, sinks_d.partition_broadcast(P)).then_inc(L["sinks"], 16)
            pl.dma_start(rb, rbias_d.partition_broadcast(P)).then_inc(L["sinks"], 16)
            pl.dma_start(grp, grp_d[:, 0:NE]).then_inc(L["sinks"], 16)
            pl.dma_start(iota, grp_d[:, NE:2 * NE]).then_inc(L["sinks"], 16)
            pl.dma_start(cm_add, cmpmask_d[:, 0:2 * NCMP]).then_inc(L["sinks"], 16)
            pl.dma_start(cm_mul, cmpmask_d[:, 2 * NCMP:4 * NCMP]).then_inc(L["sinks"], 16)
            pl.wait_ge(W["act_lo_ready"], split_end("x"))
            for slot in range(2):
                nc.gpsimd.memset(pool[0:64, SC1[2] + 2 * slot, 64:P], NEG)
                ins = nc.gpsimd.memset(pool[0:64, SC1[2] + 1 + 2 * slot, 192:S], NEG)
            ins.then_inc(W["masks_set"], 1)
            attend(MEM_UNITS, 0, SC1)
            attend(LOCAL_UNITS, 4, SC1)
            pl.wait_ge(W["merged_ready"], HC)
            pl.dma_start(chunks(H, DC), x_d).then_inc(L["x_again"], 16)
            pl.wait_ge(W["act_lo_ready"], split_end("merged"))
            pl.dma_start(flat(GDRAW, 2)[:, 0:384], gd_d).then_inc(L["gd"], 16)
            pl.wait_ge(W["act_lo_ready"], split_end("ffn"))
            for s in range(4):
                pl.dma_start(flat(ADA[s], 8), ada_tiles[s]).then_inc(ada_landed[s], 16)
            added = Tally(W["ada_added"])

            def ada_group(g, loads):
                acc = flat(ADACC, 4)
                for j in range(8):
                    parts = [flat(ADA[j % 4] + 4 * r, 4) for r in range(2)]
                    pl.wait_ge(W["ada_scaled"], 8 * g + (j + 1))
                    if j == 0:
                        if not isinstance(g, int) or g > 0:
                            pl.wait_ge(W["ada_sums"], g)
                        ins = nc.gpsimd.tensor_tensor(acc, parts[0], parts[1], ALU.add)
                    else:
                        pl.wait_ge(added.sem, added.add(nc.gpsimd.tensor_tensor(acc, acc, parts[0], ALU.add)))
                        ins = nc.gpsimd.tensor_tensor(acc, acc, parts[1], ALU.add)
                    ins.then_inc(W["ada_used"], 1)
                    pl.wait_ge(W["ada_used"], 8 * g + (j + 1))
                    if j + 4 < 8 or loads:
                        pl.dma_start(flat(ADA[j % 4], 8), ada_tiles[8 * g + (j + 4)])\
                            .then_inc(ada_landed[j % 4], 16)

            ada_group(0, True)
            with pl.Fori(0, G1 - 2) as i:
                with added.loop(i, 7, G1 - 2):
                    ada_group(i + 1, True)
            ada_group(G1 - 1, False)
            pl.wait_ge(W["ada_used"], 8 * G1)
            pl.dma_start(flat(Q2, 1)[0:32, 0:32], tab_d).then_inc(L["tables"], 16)
            pl.dma_start(flat(Q2 + 1, 2)[0:32, :], onehot_d).then_inc(L["tables"], 16)
            pl.dma_start(flat(Q2 + 3, 2)[0:32, :], maskrow_d).then_inc(L["tables"], 16)
            pl.wait_ge(W["hidden_lo"], G1)
            pl.dma_start(flat(28, 1)[:, 0:64], w2_d[0]).then_inc(L["cmp"], 16)
            pl.dma_start(flat(28, 1)[:, 64:P], w2_d[0]).then_inc(L["cmp"], 16)
            pl.dma_start(flat(28, 1)[:, P:P + 64], w2_d[1]).then_inc(L["cmp"], 16)
            for j in range(2):
                pl.dma_start(flat(29, 1)[64 * j:64 * j + 64, 0:64], pe_d).then_inc(L["cmp"], 16)
            pl.wait_ge(W["bias_rows_copied"], 1)
            pl.dma_start(fbias_d, flat(ROWS, 2)[0:32, :].unsqueeze(1).to_broadcast([32, P, 512])).then_inc(W["bias_rows_stored"], 16)
            pl.wait_ge(W["bias_rows_stored"], 16)
            pl.wait_ge(W["act_lo_ready"], split_end("norm1"))
            for n in range(4):
                wait(pl, W["cmp_hidden"], n)
                for j in range(2):
                    pl.dma_start(flat(W1, 8)[64 * j:64 * j + 64, :], w1_d[n]).then_inc(L["w1"], 16)
            attend(SECOND_UNITS, 20, SC2)
            pl.wait_ge(W["head_out"], 52)
            pl.dma_start(flat(RRAW, 1)[:, 0:256], router_d).then_inc(L["router"], 16)
            pl.wait_ge(W["act_lo_ready"], split_end("norm2"))
            nc.gpsimd.memset(chunks(Y, DC), 0.0).then_inc(W["y_ready"], 1)
            pl.wait_ge(W["combine_copied"], 1)
            pl.dma_start(comb_d, pool[0:NE, RRAW + 2, :]).then_inc(W["combine_stored"], 16)
            pl.wait_ge(W["combine_stored"], 16)
            pl.dma_start(chunks(COMB, NE), comb_d.partition_broadcast(P)).then_inc(L["comb"], 16)
            pl.wait_ge(L["comb"], 16)
            acc = flat(ADACC_LAST, 4)
            for j in range(8):
                pl.dma_start(flat(ADA_LAST, 8), ada_tiles[8 * G1 + j]).then_inc(ada_landed[j % 4], 16)
                pl.wait_ge(ada_landed[j % 4], 32 * G1 + 16 * (j // 4 + 1))
                for r in range(2):
                    part, c = flat(ADA_LAST + 4 * r, 4), cact[:, 2 * j + r:2 * j + r + 1]
                    if j == 0 and r == 0:
                        pl.wait_ge(added.sem, added.add(nc.gpsimd.tensor_scalar(acc, part, c, 1.0, ALU.mult, ALU.mult)))
                        continue
                    pl.wait_ge(added.sem, added.add(nc.gpsimd.tensor_scalar(part, part, c, 1.0, ALU.mult, ALU.mult)))
                    ins = nc.gpsimd.tensor_tensor(acc, acc, part, ALU.add)
                    if r == 0:
                        pl.wait_ge(added.sem, added.add(ins))
                ins.then_inc(W["ada_used"], 1)
                pl.wait_ge(W["ada_used"], 8 * G1 + j + 1)


SMALL_LOADS = 6
INPUTS = ["tiles", "ada_tiles", "x", "mem", "params", "rel_rev", "onehot", "maskrow", "ident", "cmpmask",
          "tab", "sinks", "rbias", "router", "gd", "w1", "w2", "pe", "grp"]


def bucket(dist):
    dist = np.maximum(dist, 0)
    large = 16 + (np.log(np.maximum(dist, 1).astype(np.float32) / np.float32(16))
                  / np.float32(np.log(2048 / 16)) * np.float32(16)).astype(np.int32)
    return np.where(dist < 16, dist, np.minimum(large, 31))


def constants():
    dist = 255 - np.arange(512)
    onehot = (bucket(dist)[None, :] == np.arange(32)[:, None]).astype(np.float32)
    causal = np.where(dist >= 0, 0.0, NEG)
    held = (dist >= 0) * ((dist <= 128).astype(int) + (dist % 4 == 0) + (dist % 16 == 0))
    dilated = np.where(held > 0, np.log(np.maximum(held, 1)), NEG)
    window = np.where((dist >= 0) & (dist <= 127), 0.0, NEG)
    maskrow = np.repeat(np.stack([dilated, window, causal, causal]), 8, axis=0).astype(np.float32)
    q = np.arange(P)[:, None, None] + P * np.arange(2)[None, :, None]
    seen = 16 * np.arange(NCMP)[None, None, :] + 31 <= q
    cmpmask = np.concatenate([np.where(seen, 0.0, NEG).reshape(P, -1), seen.reshape(P, -1)], axis=1)
    grp = np.tile(np.concatenate([np.arange(NE) // 4, np.arange(NE)]), (P, 1))
    return dict(onehot=onehot, maskrow=maskrow, ident=np.eye(P, dtype=np.float32),
                cmpmask=cmpmask.astype(np.float32), grp=grp.astype(np.float32))


def layout(a):
    def chunk_cols(v):
        return v.reshape(-1, P).T

    def fm(x):
        return np.ascontiguousarray(x.T.reshape(-1, P, x.shape[0]).transpose(1, 0, 2))

    def cut(w, kc, nc_):
        k, n = w.shape
        t = w.reshape(k // (kc * P), kc, P, n // (nc_ * P), nc_, P)
        return t.transpose(3, 0, 2, 4, 1, 5).reshape(-1, P, 2048)

    def token_major(w):
        return np.concatenate([w[:, n:n + 512].reshape(4, 4, P, 512).transpose(0, 2, 1, 3).reshape(4, P, 2048)
                               for n in range(0, w.shape[1], 512)])

    def down(w):
        k, n = w.shape
        t = w.reshape(k // 512, 4, P, n // 512, 4, P)
        return t.transpose(0, 3, 2, 4, 1, 5).reshape(-1, P, 2048)

    def pairs(a_, b_):
        return np.stack([a_, b_], axis=1).reshape(-1, P, 2048)

    def grouped(up, dn):
        n = len(dn) // 4
        up, dn = up.reshape(n, 8, P, 2048), dn.reshape(n, 4, P, 2048)
        parts = [up[0]]
        for g in range(1, n):
            parts += [up[g, 0:4], dn[g - 1], up[g, 4:8]]
        return parts + [dn[n - 1]]

    a = {k: np.asarray(v) for k, v in a.items()}
    w_in = a["w_in"][0]
    kv = a["w_mem_kv"][0]
    t = cut(w_in, 16, 1)
    ca, cg, q, k, qm, gates = t[0:8], t[8:16], t[16:24], t[24:32], t[40:48], t[48:96]
    v = token_major(w_in[:, 4 * HALF:5 * HALF])
    up = cut(a["w_up"][0], 16, 1)
    two = a["w_in_2"][0]
    o = np.cumsum([0, 512, 512, 512, 512, 128, 128, 512, 512, 512, 512, 128, 128, 128, 128, 128, 128, 24])
    part = [two[:, o[n]:o[n + 1]] for n in range(17)]

    def heads(w):
        return w.reshape(D, 8, 64)[:, KV_ORDER].reshape(D, 512)

    def rows(w):
        w = w.reshape(4, 8, 64, -1).copy()
        for m in (1, 3):
            w[m] = w[m][KV_ORDER]
        return w.reshape(D, -1)

    second = np.concatenate([part[0], heads(part[3]), part[6], heads(part[9]), part[1], part[7], part[4], part[10],
                             part[12], part[14], part[11], part[5], part[13], part[15]], axis=1)
    eg, eu, ed = a["exp_w_gate_2"][0], a["exp_w_up_2"][0], a["exp_w_down_2"][0]
    experts = np.concatenate([pairs(cut(eg[e], 16, 1), cut(eu[e], 16, 1)) for e in range(NE)])
    out = dict()
    out["tiles"] = np.concatenate(
        [cut(kv[:, :HALF], 16, 1), token_major(kv[:, HALF:]), qm, q, k, v, pairs(cg, ca), gates, cut(a["w_attn_out"][0], 8, 2), cut(a["w_mem_out"][0], 8, 2),
         cut(a["w_conv_out"][0], 8, 2), cut(a["w_o"][0], 16, 1)]
        + grouped(pairs(up[0:FC], up[FC:]), down(a["w_down"][0]))
        + [cut(second, 16, 1), token_major(np.concatenate([part[2], part[8]], axis=1)), cut(rows(a["w_out_2"][0]), 16, 1)]
        + grouped(experts, down(ed.reshape(NE * 512, D))))
    assert out["tiles"].shape == (NT, P, 2048)
    ada = a["ada_w_2"][0].reshape(8, 2, P, 12, 1024)
    out["ada_tiles"] = ada.transpose(3, 0, 2, 1, 4).reshape(96, P, 2048)
    out["x"], out["mem"] = fm(a["x"][0]), fm(a["mem"][0])
    by_name = dict(
        mem_norm_g=a["mem_norm_g"], mix_norm_g=a["mix_norm_g"], ffn_norm_g=a["ffn_norm_g"],
        final_norm_g=a["final_norm_g"], norm1_g=a["norm1_g_2"], norm2_g=a["norm2_g_2"],
        mix2_g=rows(a["mix_norm_g_2"][0].reshape(D, 1)), final2_g=a["final_g_2"], gate_b=a["gate_b"],
        conv_b=a["conv_b"], ln_g=a["conv_ln_g"], ln_b=a["conv_ln_b"], ada_b=a["ada_b_2"], c=a["c_2"],
        fconv_w=a["ffn_conv_w"][0].reshape(3, 2, FC, P).transpose(0, 2, 1, 3),
        fconv_b=a["ffn_conv_b"][0].reshape(2, FC, P).transpose(1, 0, 2), conv_w=a["conv_w"])
    out["params"] = np.concatenate([chunk_cols(by_name[n].reshape(-1)) for n, _ in PARAMS], axis=1)
    out["rel_rev"] = np.tile(a["rel_bias"][0][:, None, ::-1], (1, 64, 1))
    out["tab"] = a["rel_bias_2"]
    out["sinks"] = a["sinks_2"][0]
    out["rbias"] = a["router_bias_2"]
    out["router"] = a["router_w_2"].reshape(DC, P, NE).transpose(1, 0, 2).reshape(P, -1)
    out["gd"] = part[16].reshape(DC, P, 24).transpose(1, 0, 2).reshape(P, -1)

    def w1(w):
        return w[0].reshape(2, 16, 64, P).transpose(0, 2, 1, 3).reshape(2, 64, 2048)

    out["w1"] = np.concatenate([w1(a["nsa_cmp_w1_k_2"]), w1(a["nsa_cmp_w1_v_2"])])
    out["w2"] = np.concatenate([a["nsa_cmp_w2_k_2"], a["nsa_cmp_w2_v_2"]])
    out["pe"] = np.concatenate([a["nsa_pe_k_2"][0].T, a["nsa_pe_v_2"][0].T], axis=1)
    out.update(constants())
    return out


def kernel(**inputs):
    import concourse.bacc as _bacc
    from concourse.bass_utils import run_bass_kernel_spmd as _run

    nc = _bacc.Bacc("TRN2", target_bir_lowering=False, num_devices=1)
    laid = layout(inputs)
    arrays, args = {}, []
    for name in INPUTS:
        arrays[name + "_dram"] = np.ascontiguousarray(laid[name])
        args.append(nc.dram_tensor(name + "_dram", laid[name].shape, F32, kind="ExternalInput").ap())
    out = nc.dram_tensor("out_dram", (P, DC, S), F32, kind="ExternalOutput").ap()
    fbias = nc.dram_tensor("bias_rows_dram", (32, P, 512), F32, kind="Internal").ap()
    comb = nc.dram_tensor("combine_dram", (NE, S), F32, kind="Internal").ap()
    build(nc, *args, out, fbias, comb)
    r = _run(nc, [arrays], core_ids=[0])
    y = r.results[0]["out_dram"]
    return y.transpose(2, 1, 0).reshape(1, S, D)
```
